# Optimizing a Trainium2 kernel written in Bass

```python
import math
import jax, jax.numpy as jnp
from jax import lax
import numpy as np

D_MODEL = 1024
BATCH = 1
SEQ = 256
DEPTH = 2

N_MIXERS = 2
DN_HEADS = 8
DN_HEAD_DIM = 128
DN_DIM = DN_HEADS * DN_HEAD_DIM
DN_CONV = 4
DN_CHUNK = 64
DN_IN = 4 * DN_DIM + 2 * DN_HEADS
MB_HEADS = 8
MB_HEAD_DIM = D_MODEL // MB_HEADS
MB_DIM = MB_HEADS * MB_HEAD_DIM
MB_BLOCK = 256
MB_TOPK = 3
MB_QCHUNK = 16
D_FF = 4 * D_MODEL
RMS_EPS = 1e-6
N_DN_LAYERS = (DEPTH + 1) // 2
N_MB_LAYERS = DEPTH // 2


def rmsnorm(x, g):
    xf = x.astype(jnp.float32)
    y = xf * lax.rsqrt(jnp.mean(xf * xf, axis=-1, keepdims=True) + RMS_EPS)
    return (y * g.astype(jnp.float32)).astype(x.dtype)

def l2norm(x):
    xf = x.astype(jnp.float32)
    return xf * lax.rsqrt(jnp.sum(xf * xf, axis=-1, keepdims=True) + 1e-6)

def causal_depthwise_conv(x, w):
    k_w = w.shape[0]
    t = x.shape[1]
    xp = jnp.pad(x, ((0, 0), (k_w - 1, 0), (0, 0)))
    y = xp[:, 0:t] * w[0]
    for j in range(1, k_w):
        y = y + xp[:, j:j + t] * w[j]
    return y

def alibi_slopes(n_heads):
    return jnp.exp2(-8.0 * jnp.arange(1, n_heads + 1, dtype=jnp.float32) / n_heads)

def chunk_gated_delta_rule(q, k, v, g, beta):
    b, h, t, dk = q.shape
    dv = v.shape[-1]
    c = DN_CHUNK
    n = t // c
    q = q.astype(jnp.float32).reshape(b, h, n, c, dk)
    k = k.astype(jnp.float32).reshape(b, h, n, c, dk)
    v = v.astype(jnp.float32).reshape(b, h, n, c, dv)
    g = g.astype(jnp.float32).reshape(b, h, n, c)
    beta = beta.astype(jnp.float32).reshape(b, h, n, c)

    gc = jnp.cumsum(g, axis=-1)
    idx = jnp.arange(c)
    tri_incl = idx[:, None] >= idx[None, :]
    tri_strict = idx[:, None] > idx[None, :]
    decay = jnp.exp(jnp.where(tri_incl, gc[..., :, None] - gc[..., None, :], -jnp.inf))

    k_beta = k * beta[..., None]
    a_low = jnp.where(tri_strict, jnp.einsum('bhncd,bhnsd->bhncs', k_beta, k) * decay, 0.0)
    a_mat = a_low + jnp.eye(c, dtype=jnp.float32)
    rhs = jnp.concatenate([v * beta[..., None], k_beta * jnp.exp(gc)[..., None]], axis=-1)
    sol = lax.linalg.triangular_solve(a_mat, rhs, left_side=True, lower=True, unit_diagonal=True)
    u, w = sol[..., :dv], sol[..., dv:]

    attn_intra = jnp.einsum('bhncd,bhnsd->bhncs', q, k) * decay
    q_dec = q * jnp.exp(gc)[..., None]
    k_dec = k * jnp.exp(gc[..., -1:] - gc)[..., None]
    g_tot = jnp.exp(gc[..., -1])

    xs = tuple(jnp.moveaxis(a, 2, 0) for a in (u, w, q_dec, k_dec, attn_intra, g_tot))

    def step(state, inp):
        u_c, w_c, qd_c, kd_c, at_c, gt_c = inp
        v_new = u_c - jnp.einsum('bhcd,bhde->bhce', w_c, state)
        o_c = jnp.einsum('bhcd,bhde->bhce', qd_c, state) + jnp.einsum('bhcs,bhse->bhce', at_c, v_new)
        state = state * gt_c[..., None, None] + jnp.einsum('bhcd,bhce->bhde', kd_c, v_new)
        return state, o_c

    s0 = jnp.zeros((b, h, dk, dv), jnp.float32)
    _, o = lax.scan(step, s0, xs)
    return jnp.moveaxis(o, 0, 2).reshape(b, h, t, dv)

def gated_deltanet(hn, w_in, conv_w, a_log, dt_bias, out_norm_g, w_out):
    b, t, _ = hn.shape
    proj = hn @ w_in
    qkv = jax.nn.silu(causal_depthwise_conv(proj[..., :3 * DN_DIM], conv_w))
    z = proj[..., 3 * DN_DIM:4 * DN_DIM]
    b_raw = proj[..., 4 * DN_DIM:4 * DN_DIM + DN_HEADS].astype(jnp.float32)
    a_raw = proj[..., 4 * DN_DIM + DN_HEADS:].astype(jnp.float32)

    def heads(a):
        return a.reshape(b, t, DN_HEADS, DN_HEAD_DIM).transpose(0, 2, 1, 3)

    q = heads(l2norm(heads(qkv[..., :DN_DIM]).transpose(0, 2, 1, 3)) * DN_HEAD_DIM ** -0.5)
    k = heads(l2norm(heads(qkv[..., DN_DIM:2 * DN_DIM]).transpose(0, 2, 1, 3)))
    v = heads(qkv[..., 2 * DN_DIM:])
    beta = jax.nn.sigmoid(b_raw).transpose(0, 2, 1)
    g = (-jnp.exp(a_log.astype(jnp.float32)) *
         jax.nn.softplus(a_raw + dt_bias.astype(jnp.float32))).transpose(0, 2, 1)
    o = chunk_gated_delta_rule(q, k, v, g, beta)
    o = o.transpose(0, 2, 1, 3).astype(hn.dtype)
    o = rmsnorm(o, out_norm_g) * jax.nn.silu(z.reshape(b, t, DN_HEADS, DN_HEAD_DIM))
    return o.reshape(b, t, DN_DIM) @ w_out

def moba_attention(q, k, v):
    b, h, t, dh = q.shape
    nb = -(-t // MB_BLOCK)
    tp = nb * MB_BLOCK
    pad = ((0, 0), (0, 0), (0, tp - t), (0, 0))
    q, k, v = jnp.pad(q, pad), jnp.pad(k, pad), jnp.pad(v, pad)
    kb = k.reshape(b, h, nb, MB_BLOCK, dh)
    vb = v.reshape(b, h, nb, MB_BLOCK, dh)
    top = min(MB_TOPK, nb)
    scale = dh ** -0.5
    slopes = alibi_slopes(h)

    k_mean = jnp.mean(kb.astype(jnp.float32), axis=3)
    gate = jnp.einsum('bhtd,bhnd->bhtn', q.astype(jnp.float32), k_mean)
    q_blk = jnp.arange(tp) // MB_BLOCK
    past = jnp.arange(nb)[None, :] < q_blk[:, None]
    gate = jnp.where(past, gate, -jnp.inf)
    _, sel = lax.top_k(gate, top)
    valid = sel < q_blk[:, None]

    n_qc = tp // MB_QCHUNK

    def to_chunks(a):
        return jnp.moveaxis(a.reshape(b, h, n_qc, MB_QCHUNK, *a.shape[3:]), 2, 0)

    gather_blocks = jax.vmap(jax.vmap(lambda blocks, ids: blocks[ids]))

    def attend_chunk(args):
        qc, selc, validc, ci = args
        t0 = ci * MB_QCHUNK
        blk = t0 // MB_BLOCK
        tpos = (t0 + jnp.arange(MB_QCHUNK)).astype(jnp.float32)
        ks = gather_blocks(kb, selc)
        vs = gather_blocks(vb, selc)
        s_sel = jnp.einsum('bhqd,bhqnld->bhqnl', qc, ks).astype(jnp.float32) * scale
        kpos_sel = (selc[..., None] * MB_BLOCK + jnp.arange(MB_BLOCK)).astype(jnp.float32)
        dist_sel = tpos[:, None, None] - kpos_sel
        s_sel = jnp.where(validc[..., None], s_sel - slopes[:, None, None, None] * dist_sel, -jnp.inf)
        ko = lax.dynamic_index_in_dim(kb, blk, axis=2, keepdims=False)
        vo = lax.dynamic_index_in_dim(vb, blk, axis=2, keepdims=False)
        s_own = jnp.einsum('bhqd,bhld->bhql', qc, ko).astype(jnp.float32) * scale
        dist_own = tpos[:, None] - (blk * MB_BLOCK + jnp.arange(MB_BLOCK)).astype(jnp.float32)
        s_own = jnp.where(dist_own >= 0, s_own - slopes[:, None, None] * dist_own, -jnp.inf)
        logits = jnp.concatenate([s_sel.reshape(b, h, MB_QCHUNK, top * MB_BLOCK), s_own], axis=-1)
        p = jax.nn.softmax(logits, axis=-1).astype(vs.dtype)
        p_sel = p[..., :top * MB_BLOCK].reshape(b, h, MB_QCHUNK, top, MB_BLOCK)
        p_own = p[..., top * MB_BLOCK:]
        return (jnp.einsum('bhqnl,bhqnld->bhqd', p_sel, vs) +
                jnp.einsum('bhql,bhld->bhqd', p_own, vo))

    out = lax.map(attend_chunk, (to_chunks(q), to_chunks(sel), to_chunks(valid), jnp.arange(n_qc)))
    out = jnp.moveaxis(out, 0, 2).reshape(b, h, tp, dh)
    return out[:, :, :t]

def moba_layer(hn, w_in, w_out):
    b, t, _ = hn.shape
    proj = hn @ w_in

    def heads(a):
        return a.reshape(b, t, MB_HEADS, MB_HEAD_DIM).transpose(0, 2, 1, 3)

    q = heads(proj[..., :MB_DIM])
    k = heads(proj[..., MB_DIM:2 * MB_DIM])
    v = heads(proj[..., 2 * MB_DIM:])
    o = moba_attention(q, k, v)
    return o.transpose(0, 2, 1, 3).reshape(b, t, MB_DIM) @ w_out

def squared_relu_mlp(hn, w_up, w_down):
    return jnp.square(jax.nn.relu(hn @ w_up)) @ w_down

def first_inputs(seed: int = 0) -> dict:
    key = jax.random.key(seed)
    ks = jax.random.split(key, 16)
    f32 = jnp.float32
    x = jax.random.normal(ks[0], (BATCH, SEQ, D_MODEL), f32)
    mix_norm_g = 1.0 + 0.02 * jax.random.normal(ks[1], (DEPTH, D_MODEL), f32)
    mlp_norm_g = 1.0 + 0.02 * jax.random.normal(ks[2], (DEPTH, D_MODEL), f32)
    dn_w_in = jax.random.normal(ks[3], (N_DN_LAYERS, D_MODEL, DN_IN), f32) * D_MODEL ** -0.5
    dn_conv_w = jax.random.normal(ks[4], (N_DN_LAYERS, DN_CONV, 3 * DN_DIM), f32) * DN_CONV ** -0.5
    dn_a_log = jnp.log(jax.random.uniform(ks[5], (N_DN_LAYERS, DN_HEADS), f32, 1.0, 16.0))
    dt = jnp.exp(jax.random.uniform(ks[6], (N_DN_LAYERS, DN_HEADS), f32, math.log(1e-3), math.log(1e-1)))
    dn_dt_bias = dt + jnp.log(-jnp.expm1(-dt))
    dn_out_norm_g = 1.0 + 0.02 * jax.random.normal(ks[7], (N_DN_LAYERS, DN_HEAD_DIM), f32)
    dn_w_out = jax.random.normal(ks[8], (N_DN_LAYERS, DN_DIM, D_MODEL), f32) * DN_DIM ** -0.5
    mb_w_in = jax.random.normal(ks[9], (N_MB_LAYERS, D_MODEL, 3 * MB_DIM), f32) * D_MODEL ** -0.5
    mb_w_out = jax.random.normal(ks[10], (N_MB_LAYERS, MB_DIM, D_MODEL), f32) * MB_DIM ** -0.5
    mlp_w_up = jax.random.normal(ks[11], (DEPTH, D_MODEL, D_FF), f32) * D_MODEL ** -0.5
    mlp_w_down = jax.random.normal(ks[12], (DEPTH, D_FF, D_MODEL), f32) * D_FF ** -0.5
    final_norm_g = 1.0 + 0.02 * jax.random.normal(ks[13], (D_MODEL,), f32)
    return {"x": x, "mix_norm_g": mix_norm_g, "mlp_norm_g": mlp_norm_g,
            "dn_w_in": dn_w_in, "dn_conv_w": dn_conv_w, "dn_a_log": dn_a_log,
            "dn_dt_bias": dn_dt_bias, "dn_out_norm_g": dn_out_norm_g, "dn_w_out": dn_w_out,
            "mb_w_in": mb_w_in, "mb_w_out": mb_w_out,
            "mlp_w_up": mlp_w_up, "mlp_w_down": mlp_w_down, "final_norm_g": final_norm_g}

def first_block(x, mix_norm_g, mlp_norm_g, dn_w_in, dn_conv_w, dn_a_log, dn_dt_bias,
              dn_out_norm_g, dn_w_out, mb_w_in, mb_w_out, mlp_w_up, mlp_w_down, final_norm_g):
    h = x
    for i in range(DEPTH):
        hn = rmsnorm(h, mix_norm_g[i])
        j = i // N_MIXERS
        if i % N_MIXERS == 0:
            mix = gated_deltanet(hn, dn_w_in[j], dn_conv_w[j], dn_a_log[j], dn_dt_bias[j],
                                 dn_out_norm_g[j], dn_w_out[j])
        else:
            mix = moba_layer(hn, mb_w_in[j], mb_w_out[j])
        h = h + mix.astype(h.dtype)
        h = h + squared_relu_mlp(rmsnorm(h, mlp_norm_g[i]), mlp_w_up[i], mlp_w_down[i])
    return rmsnorm(h, final_norm_g)


DEPTH_2 = 1

CHUNK = 64
Q_BLOCK = 128
MEM_LEN = 256
HEAD_DIM = 64
BR_W = 512
N_BRANCH = 4
A_HEADS = BR_W // (2 * HEAD_DIM)
F_HEADS = BR_W // HEAD_DIM
CONV_W = BR_W
CONV_K = 31
SC_W = BR_W
SC_K = 3
IN_COLS = 3 * BR_W + (3 * BR_W + F_HEADS) + 2 * CONV_W + 3 * SC_W
X_HEADS = 4
X_HEAD_DIM = 128
X_W = X_HEADS * X_HEAD_DIM
D_FF_2 = 2816
FFN_K = 3
EPS = 1e-6


def _rms_norm(x, g):
    xf = x.astype(jnp.float32)
    y = xf * lax.rsqrt(jnp.mean(xf * xf, axis=-1, keepdims=True) + EPS)
    return (y * g.astype(jnp.float32)).astype(x.dtype)

def _layer_norm(x, g, b):
    xf = x.astype(jnp.float32)
    mu = jnp.mean(xf, axis=-1, keepdims=True)
    var = jnp.mean(jnp.square(xf - mu), axis=-1, keepdims=True)
    y = (xf - mu) * lax.rsqrt(var + EPS)
    return (y * g.astype(jnp.float32) + b.astype(jnp.float32)).astype(x.dtype)

def _dwconv_causal(x, w):
    K, C = w.shape
    return lax.conv_general_dilated(x, w[:, None, :].astype(x.dtype), window_strides=(1,),
                                    padding=[(K - 1, 0)], dimension_numbers=('NWC', 'WIO', 'NWC'),
                                    feature_group_count=C)

def _diff_attention(q, k, v, lam, t_pos):
    B, S, H = q.shape[:3]
    nb = S // Q_BLOCK
    scale = HEAD_DIM ** -0.5
    qb = q.reshape(B, nb, Q_BLOCK, H, 2, HEAD_DIM).transpose(1, 0, 2, 3, 4, 5)
    tq = t_pos.reshape(nb, Q_BLOCK)
    k_chunk = t_pos // CHUNK

    def one(args):
        q_blk, tq_blk = args
        s = jnp.einsum('bqhcd,bkhcd->bhcqk', q_blk, k, preferred_element_type=jnp.float32) * scale
        mask = k_chunk[None, :] <= (tq_blk // CHUNK)[:, None]
        p = jax.nn.softmax(jnp.where(mask, s, -jnp.inf), axis=-1)
        a = p[:, :, 0] - lam * p[:, :, 1]
        return jnp.einsum('bhqk,bkhe->bqhe', a.astype(v.dtype), v)

    o = lax.map(one, (qb, tq))
    return o.transpose(1, 0, 2, 3, 4).reshape(B, S, H, 2 * HEAD_DIM)

def _forgetting_attention(q, k, v, log_f, t_pos):
    B, S, H = q.shape[:3]
    nb = S // Q_BLOCK
    scale = HEAD_DIM ** -0.5
    c = jnp.cumsum(log_f.astype(jnp.float32), axis=1)
    c_k = c.transpose(0, 2, 1)
    qb = q.reshape(B, nb, Q_BLOCK, H, HEAD_DIM).transpose(1, 0, 2, 3, 4)
    cb = c.reshape(B, nb, Q_BLOCK, H).transpose(1, 0, 3, 2)
    tq = t_pos.reshape(nb, Q_BLOCK)

    def one(args):
        q_blk, c_blk, tq_blk = args
        s = jnp.einsum('bqhd,bkhd->bhqk', q_blk, k, preferred_element_type=jnp.float32) * scale
        s = s + c_blk[..., None] - c_k[:, :, None, :]
        mask = t_pos[None, :] <= tq_blk[:, None]
        p = jax.nn.softmax(jnp.where(mask, s, -jnp.inf), axis=-1)
        return jnp.einsum('bhqk,bkhd->bqhd', p.astype(v.dtype), v)

    o = lax.map(one, (qb, cb, tq))
    return o.transpose(1, 0, 2, 3, 4).reshape(B, S, H * HEAD_DIM)

def second_inputs(seed: int = 0) -> dict:
    key = jax.random.key(seed)
    ks = iter(jax.random.split(key, 48))
    L, D = DEPTH_2, D_MODEL

    def nrm(shape, scale):
        return jax.random.normal(next(ks), shape, jnp.float32) * scale

    def gain(shape):
        return 1.0 + nrm(shape, 0.05)

    return {
        "x": nrm((BATCH, SEQ, D), 1.0),
        "mem": nrm((BATCH, MEM_LEN, D), 1.0),
        "norm_mix_pre": gain((L, D)),
        "norm_mix_post": gain((L, D)),
        "w_in": nrm((L, D, IN_COLS), D ** -0.5),
        "b_fgt": 2.0 + nrm((L, F_HEADS), 0.1),
        "lam_q1": nrm((L, HEAD_DIM), 0.1),
        "lam_k1": nrm((L, HEAD_DIM), 0.1),
        "lam_q2": nrm((L, HEAD_DIM), 0.1),
        "lam_k2": nrm((L, HEAD_DIM), 0.1),
        "diff_norm": gain((L, 2 * HEAD_DIM)),
        "b_glu": nrm((L, 2 * CONV_W), 0.02),
        "conv_dw": nrm((L, CONV_K, CONV_W), CONV_K ** -0.5),
        "conv_dw_b": nrm((L, CONV_W), 0.02),
        "conv_ln_g": gain((L, CONV_W)),
        "conv_ln_b": nrm((L, CONV_W), 0.02),
        "sc_w": nrm((L, SC_K, SC_W), SC_K ** -0.5),
        "w_branch": nrm((L, N_BRANCH, BR_W, D), BR_W ** -0.5),
        "w_gate": nrm((L, D, N_BRANCH * D), D ** -0.5),
        "b_gate": nrm((L, N_BRANCH * D), 0.02),
        "w_out": nrm((L, D, D), D ** -0.5),
        "norm_x_pre": gain((L, D)),
        "norm_x_post": gain((L, D)),
        "norm_mem": gain((L, D)),
        "w_xq": nrm((L, D, X_W), D ** -0.5),
        "w_xkv": nrm((L, D, 2 * X_W), D ** -0.5),
        "w_xo": nrm((L, X_W, D), X_W ** -0.5),
        "norm_ffn_pre": gain((L, D)),
        "norm_ffn_post": gain((L, D)),
        "w_up": nrm((L, D, 2 * D_FF_2), D ** -0.5),
        "ffn_dw": nrm((L, FFN_K, 2 * D_FF_2), FFN_K ** -0.5),
        "ffn_dw_b": nrm((L, 2 * D_FF_2), 0.02),
        "w_down": nrm((L, D_FF_2, D), D_FF_2 ** -0.5),
    }

def second_block(x, mem, norm_mix_pre, norm_mix_post, w_in, b_fgt, lam_q1, lam_k1, lam_q2, lam_k2,
              diff_norm, b_glu, conv_dw, conv_dw_b, conv_ln_g, conv_ln_b, sc_w, w_branch, w_gate,
              b_gate, w_out, norm_x_pre, norm_x_post, norm_mem, w_xq, w_xkv, w_xo, norm_ffn_pre,
              norm_ffn_post, w_up, ffn_dw, ffn_dw_b, w_down):
    B, S, D = x.shape
    t_pos = jnp.arange(S, dtype=jnp.int32)
    sizes = [BR_W, BR_W, BR_W, BR_W, BR_W, BR_W, F_HEADS, 2 * CONV_W, SC_W, SC_W, SC_W]
    cuts = [int(v) for v in np.cumsum(sizes)[:-1]]

    for l in range(DEPTH_2):
        h = _rms_norm(x, norm_mix_pre[l])
        (a_q, a_k, a_v, f_q, f_k, f_v, f_g, c_u, s_x, s_b, s_c) = jnp.split(h @ w_in[l], cuts, axis=-1)

        lambda_init = 0.8 - 0.6 * math.exp(-0.3 * l)
        lam = (jnp.exp(jnp.sum(lam_q1[l].astype(jnp.float32) * lam_k1[l].astype(jnp.float32)))
               - jnp.exp(jnp.sum(lam_q2[l].astype(jnp.float32) * lam_k2[l].astype(jnp.float32))) + lambda_init)
        ya = _diff_attention(a_q.reshape(B, S, A_HEADS, 2, HEAD_DIM), a_k.reshape(B, S, A_HEADS, 2, HEAD_DIM),
                             a_v.reshape(B, S, A_HEADS, 2 * HEAD_DIM), lam, t_pos)
        ya = (_rms_norm(ya, diff_norm[l]) * (1.0 - lambda_init)).reshape(B, S, BR_W)

        log_f = jax.nn.log_sigmoid(f_g.astype(jnp.float32) + b_fgt[l].astype(jnp.float32))
        yf = _forgetting_attention(f_q.reshape(B, S, F_HEADS, HEAD_DIM), f_k.reshape(B, S, F_HEADS, HEAD_DIM),
                                   f_v.reshape(B, S, F_HEADS, HEAD_DIM), log_f, t_pos)

        c_a, c_g = jnp.split(c_u + b_glu[l], 2, axis=-1)
        yc = _dwconv_causal(c_a * jax.nn.sigmoid(c_g), conv_dw[l]) + conv_dw_b[l]
        yc = jax.nn.silu(_layer_norm(yc, conv_ln_g[l], conv_ln_b[l]))

        ys = s_b * _dwconv_causal(s_c * s_x, sc_w[l])

        br = jnp.stack([ya, yf, yc, ys], axis=2)
        proj = jnp.einsum('bsnc,ncd->bsnd', br, w_branch[l])
        gates = jax.nn.sigmoid(h @ w_gate[l] + b_gate[l]).reshape(B, S, N_BRANCH, D)
        mixed = jnp.sum(gates * proj, axis=2) @ w_out[l]
        x = x + _rms_norm(mixed, norm_mix_post[l])

        hx = _rms_norm(x, norm_x_pre[l])
        m = _rms_norm(mem, norm_mem[l])
        xq = (hx @ w_xq[l]).reshape(B, S, X_HEADS, X_HEAD_DIM)
        xk, xv = jnp.split(m @ w_xkv[l], 2, axis=-1)
        xk = xk.reshape(B, MEM_LEN, X_HEADS, X_HEAD_DIM)
        xv = xv.reshape(B, MEM_LEN, X_HEADS, X_HEAD_DIM)
        sx = jnp.einsum('bqhd,bkhd->bhqk', xq, xk, preferred_element_type=jnp.float32) * (X_HEAD_DIM ** -0.5)
        px = jax.nn.softmax(sx, axis=-1).astype(xv.dtype)
        ox = jnp.einsum('bhqk,bkhd->bqhd', px, xv).reshape(B, S, X_W) @ w_xo[l]
        x = x + _rms_norm(ox, norm_x_post[l])

        hf = _rms_norm(x, norm_ffn_pre[l])
        u = _dwconv_causal(hf @ w_up[l], ffn_dw[l]) + ffn_dw_b[l]
        u_g, u_v = jnp.split(u, 2, axis=-1)
        yff = (jax.nn.silu(u_g) * u_v) @ w_down[l]
        x = x + _rms_norm(yff, norm_ffn_post[l])

    return x


def setup_inputs(seed=0):
    out = dict(first_inputs(seed))
    for name, value in second_inputs(seed + 1).items():
        if name != "x":
            out[name + "_2"] = value
    return out


def reference(
    x, mix_norm_g, mlp_norm_g, dn_w_in, dn_conv_w, dn_a_log, dn_dt_bias, dn_out_norm_g,
    dn_w_out, mb_w_in, mb_w_out, mlp_w_up, mlp_w_down, final_norm_g, mem_2, norm_mix_pre_2,
    norm_mix_post_2, w_in_2, b_fgt_2, lam_q1_2, lam_k1_2, lam_q2_2, lam_k2_2, diff_norm_2,
    b_glu_2, conv_dw_2, conv_dw_b_2, conv_ln_g_2, conv_ln_b_2, sc_w_2, w_branch_2, w_gate_2,
    b_gate_2, w_out_2, norm_x_pre_2, norm_x_post_2, norm_mem_2, w_xq_2, w_xkv_2, w_xo_2,
    norm_ffn_pre_2, norm_ffn_post_2, w_up_2, ffn_dw_2, ffn_dw_b_2, w_down_2,
):
    x = first_block(
        x, mix_norm_g, mlp_norm_g, dn_w_in, dn_conv_w, dn_a_log, dn_dt_bias, dn_out_norm_g,
        dn_w_out, mb_w_in, mb_w_out, mlp_w_up, mlp_w_down, final_norm_g,
    )
    return second_block(
        x, mem_2, norm_mix_pre_2, norm_mix_post_2, w_in_2, b_fgt_2, lam_q1_2, lam_k1_2,
        lam_q2_2, lam_k2_2, diff_norm_2, b_glu_2, conv_dw_2, conv_dw_b_2, conv_ln_g_2,
        conv_ln_b_2, sc_w_2, w_branch_2, w_gate_2, b_gate_2, w_out_2, norm_x_pre_2,
        norm_x_post_2, norm_mem_2, w_xq_2, w_xkv_2, w_xo_2, norm_ffn_pre_2, norm_ffn_post_2,
        w_up_2, ffn_dw_2, ffn_dw_b_2, w_down_2,
    )


_drawn_inputs = setup_inputs


def setup_inputs(seed=0):
    import zlib

    import numpy as np

    out = dict(_drawn_inputs(seed))
    spreads = {}
    factors = {'dn_out_norm_g': 3.51,
     'b_fgt_2': 33.992,
     'lam_q1_2': 7.963,
     'lam_k1_2': 5.698,
     'lam_k2_2': 5.034,
     'diff_norm_2': 2.888,
     'b_glu_2': 8.0,
     'conv_dw_b_2': 4.078,
     'conv_ln_g_2': 2.929,
     'conv_ln_b_2': 8.0,
     'b_gate_2': 8.0,
     'ffn_dw_b_2': 3.634,
     'mlp_norm_g': 2.805}
    for name, (base, spread) in spreads.items():
        noise = np.random.default_rng([zlib.crc32(name.encode()), seed]).standard_normal(out[name].shape)
        drawn = base * np.exp(spread * noise) if base else spread * noise
        out[name] = __import__('jax').numpy.asarray(drawn.astype(out[name].dtype))
    for name, factor in factors.items():
        out[name] = (out[name] * factor).astype(out[name].dtype)
    return out
```

```python
from contextlib import ExitStack

import concourse.bass as bass
from concourse import mybir

F32 = mybir.dt.float32
F32R = mybir.dt.float32r
I32 = mybir.dt.int32
ALU = mybir.AluOpType
ACT = mybir.ActivationFunctionType
AX = mybir.AxisListType.X

P = 128
T = 256
NT = T // P
D = 1024
KT = D // P
RING = 4
RAW = 2
AHEAD = 3
UNIT = 2048
NEG = -1.0e30
EPS = 1e-6


class Mark:

    def __init__(self, sem, value, step=0):
        self.sem, self.value, self.step = sem, value, step
        self.done = (sem, value)

    def at(self, i):
        return self.value + self.step * i if self.step else self.value


class Signal:

    def __init__(self, sem):
        self.sem, self.count = sem, 0

    def next(self):
        self.count += 1
        return Mark(self.sem, self.count)

    def many(self, n):
        return [self.next() for _ in range(n)]

    def loop(self, iterations, n):
        out = [Mark(self.sem, self.count + k + 1, n) for k in range(n)]
        self.count += n * iterations
        return out


class Use:

    def __init__(self, bank, n, step=0):
        self.bank, self.n, self.step, self.ps = bank, n, step, bank.ps
        self.filled, self.freed = bank.filled, bank.freed
        self.done = (bank.freed, n + 1)

    def at(self, i):
        return self.n + self.step * i if self.step else self.n


class Bank:
    def __init__(self, ps, filled, freed):
        self.ps, self.filled, self.freed, self.count = ps, filled, freed, 0

    def use(self):
        self.count += 1
        return Use(self, self.count - 1)

    def loop(self, iterations, n):
        out = [Use(self, self.count + k, n) for k in range(n)]
        self.count += n * iterations
        return out


class Own:

    def __init__(self, sem):
        self.sem, self.n = sem, 0

    def add(self, k):
        self.n += k
        return k


class Part:

    def __init__(self, pe=None, act=None, dve=None, pool=None, acc=None, ready=None, parts=None,
                 uba=None, uss=None, squares=None, on_d=None, y=None, pe_cum=None, dve_cum=None,
                 uc=None, last=None):
        self.pe, self.act, self.dve, self.pool = pe, act, dve, pool
        self.acc, self.ready, self.parts = acc, ready, parts
        self.uba, self.uss, self.squares, self.on_d, self.y = uba, uss, squares, on_d, y
        self.pe_cum, self.dve_cum, self.uc, self.last = pe_cum, dve_cum, uc, last


class Block:

    def __init__(self, U, use=None, dst=None, tokens=False, scale=1.0, uses=None):
        self.U, self.use, self.dst, self.tokens, self.scale, self.uses = U, use, dst, tokens, scale, uses


class Norm:

    def __init__(self, act_tile, dve_before, dve_after, pool_tile, g, pe=None, act_parts=None, dve_parts=None,
                 parts=None, ready=None):
        self.act_tile, self.dve_before, self.dve_after = act_tile, dve_before, dve_after
        self.pool_tile, self.g = pool_tile, g
        self.pe, self.act_parts, self.dve_parts = pe, act_parts, dve_parts
        self.parts, self.ready = parts, ready


class Attention:

    def __init__(self, e, scores, max, exp, normalise, turn, turned, values, y_hi, y_lo, diff, ready,
                 squares=None, root=None, scaled=None, turn_y=None):
        self.e, self.diff, self.ready = e, diff, ready
        self.scores, self.turn, self.values, self.turn_y = scores, turn, values, turn_y
        self.exp, self.turned, self.squares, self.y_hi = exp, turned, squares, y_hi
        self.max, self.normalise, self.scaled, self.y_lo = max, normalise, scaled, y_lo
        self.root = root


def build(nc, A, out):
    ctx = ExitStack()
    with ctx:
        def sb(name, shape, dt=F32, c=ctx):
            return c.enter_context(nc.sbuf_tensor(name, shape, dt))

        def sem(name):
            return ctx.enter_context(nc.semaphore(name))

        raw = sb("raw", [P, RAW, UNIT])
        whi = sb("whi", [P, RING, UNIT], F32R)
        wlo = sb("wlo", [P, RING, UNIT], F32R)
        xhi = sb("xhi", [P, KT, T], F32R)
        xlo = sb("xlo", [P, KT, T], F32R)
        hhi = sb("hhi", [P, 2, 2, T], F32R)
        hlo = sb("hlo", [P, 2, 2, T], F32R)
        h = sb("h", [P, NT, D])
        gain = sb("gain", [P, 2, D])
        smh = sb("smh", [P, KT, 16], F32R)
        sml = sb("sml", [P, KT, 16], F32R)
        smr = sb("smr", [P, KT, 16])
        ident = sb("ident", [P, P])
        ones = sb("ones", [P, P])
        nones = sb("nones", [P, P])
        upper = sb("upper", [P, P])
        masks = sb("masks", [P, 768])
        amask = masks[:, 0:384]
        fmask = masks[:, 384:768]
        dn_lower = sb("dn_lower", [P, P])
        smo = sb("smo", [P, 64])
        sm = sb("sm", [P, 256])
        
        pool_product = sb("pool_product", [P, 2, 1, T])
        common = sb("common", [P, 9848])
        dn_ctx = ExitStack()
        with dn_ctx:
            extra = sb("dn_extra", [P, 8192], F32, dn_ctx)
        bhi = sb("bhi", [P, 16, T], F32R)
        blo = sb("blo", [P, 16, T], F32R)

        banks = []
        for b in range(8):
            ps = ctx.enter_context(nc.psum_tensor(f"bank{b}", [P, 512], F32))
            banks.append(Bank(ps, sem(f"filled{b}"), sem(f"freed{b}")))
        G, O = banks[:4], banks[4:]

        raw_in = [sem(f"raw_in{s}") for s in range(RAW)]
        hi_ready, lo_ready, unit_begun = sem("hi_ready"), sem("lo_ready"), sem("unit_begun")
        const_in = sem("const_in")
        consts_built = sem("consts_built")
        pool_self = Own(sem("pool_self"))
        act_self = Own(sem("act_self"))
        dve_self = Own(sem("dve_self"))
        hid_sq = Signal(sem("hid_sq"))
        hid_f32 = Signal(sem("hid_f32"))
        hid_lo = Signal(sem("hid_lo"))
        h_ready = Signal(sem("h_ready"))
        norm_kinds = [[Signal(sem(f"{kind}_{what}")) for what in ("sums", "means", "roots")]
                      for kind in ("turned", "product", "in_place")]
        xn_ready = Signal(sem("xn_ready"))
        x_hi = Signal(sem("x_hi"))
        gain_in = [sem("gain_in0"), sem("gain_in1")]
        mem_in = sem("mem_in")
        a2d = Signal(sem("a2d"))
        d2a = Signal(sem("d2a"))
        d2p = Signal(sem("d2p"))
        p2d = Signal(sem("p2d"))
        a2p = Signal(sem("a2p"))
        d2t = Signal(sem("d2t"))
        a2t = Signal(sem("a2t"))
        p2t = Signal(sem("p2t"))
        out_done = sem("out_done")

        def f32(ap):
            return ap.bitcast(F32)

        def bc3(ap, n):
            return ap.unsqueeze(1).broadcast_to((P, n, ap.shape[1]))

        stream = []
        state = {"U": 0}

        def features(W, col, row=0):
            if isinstance(col, int):
                return W[row:row + D, col:col + 256].rearrange("(k p) n -> p k n", p=P)
            return W[row:row + D, bass.ds(col, 256)].rearrange("(k p) n -> p k n", p=P)

        def rows(W, row):
            if isinstance(row, int):
                return W[row:row + 256, :].rearrange("(k p) n -> p k n", p=P)
            return W[bass.ds(row, 256), :].rearrange("(k p) n -> p k n", p=P)

        def unit(src):
            stream.append(("unit", state["U"], src))
            state["U"] += 1
            return state["U"] - 1

        def unit_loop(iterations, srcs):
            assert len(srcs) % RING == 0
            stream.append(("loop", state["U"], iterations, srcs))
            U = state["U"]
            state["U"] += iterations * len(srcs)
            return [U + k for k in range(len(srcs))]

        def at_unit(U, n, i):
            return U + n * i if n else U

        def load(sp, U, src, n=0, i=0):
            s = U % RAW
            if U >= RAW:
                sp.wait_ge(lo_ready, at_unit(U - RAW + 1, n, i))
            dst = raw[:, s, :]
            if len(src.shape) == 3:
                dst = dst.rearrange("p (k n) -> p k n", k=src.shape[1])
            sp.dma_start(dst, src).then_inc(raw_in[s], 16)

        def split_hi(act, U, n=0, i=0):
            V = U + AHEAD
            if not n and V >= total_units:
                return
            s = V % RING
            r = V % RAW
            act.wait_ge(raw_in[r], 16 * (V // RAW + 1) + (16 * (n // RAW) * i if n else 0))
            if V >= RING:
                act.wait_ge(unit_begun, at_unit(V - RING + 2, n, i))
            nc.scalar.activation(whi[:, s, :], raw[:, r, :], ACT.Copy).then_inc(hi_ready, 1)

        def split_lo(dve, U, n=0, i=0):
            V = U + AHEAD
            if not n and V >= total_units:
                return
            s = V % RING
            dve.wait_ge(hi_ready, at_unit(V + 1, n, i))
            nc.vector.tensor_tensor(wlo[:, s, :], raw[:, V % RAW, :], f32(whi[:, s, :]),
                                    ALU.subtract).then_inc(lo_ready, 1)

        def mm3(pe, o, shi, slo, mhi, mlo, first, last, begins_unit=False):
            ins = pe.matmul(o, shi, mhi, start=first, stop=False, skip_group_check=True)
            if begins_unit:
                ins.then_inc(unit_begun, 1)
            pe.matmul(o, shi, mlo, start=False, stop=False, skip_group_check=True)
            return pe.matmul(o, slo, mhi, start=False, stop=last, skip_group_check=True)

        psum_ss = sb("psum_ss", [P, 4])
        sm_hi, sm_lo = Signal(sem("sm_hi")), Signal(sem("sm_lo"))

        def wview(w, s, k):
            return w[:, s, :].rearrange("p (k n) -> p k n", k=k)

        def gemm_features(pe, U, use, ahi, alo, n=0, i=0, kts=KT, wk0=0, begins=True):
            s = U % RING
            pe.wait_ge(lo_ready, at_unit(U + 1, n, i))
            if use.n:
                pe.wait_ge(use.freed, use.at(i))
            wh, wl = wview(whi, s, KT), wview(wlo, s, KT)
            for f in range(2):
                for k in range(kts):
                    fs = slice(f * P, (f + 1) * P)
                    ins = mm3(pe, use.ps[:, f * T:(f + 1) * T], wh[:, wk0 + k, fs], wl[:, wk0 + k, fs],
                              ahi[:, k, :], alo[:, k, :], f == 0 and k == 0,
                              f == 1 and k == kts - 1, begins and f == 0 and k == 0)
            ins.then_inc(use.filled, 1)

        def features_part(pe, U, use, ahi, alo, first, last):
            s = U % RING
            if first == 0:
                pe.wait_ge(lo_ready, U + 1)
                if use.n:
                    pe.wait_ge(use.freed, use.n)
            wh, wl = wview(whi, s, KT), wview(wlo, s, KT)
            for n in range(first, last):
                f, k = n // KT, n % KT
                fs = slice(f * P, (f + 1) * P)
                ins = mm3(pe, use.ps[:, f * T:(f + 1) * T], wh[:, k, fs], wl[:, k, fs], ahi[:, k, :], alo[:, k, :],
                          n == 0, n == 2 * KT - 1, n == 0)
            if last == 2 * KT:
                ins.then_inc(use.filled, 1)

        def gemm_tokens(pe, U, use, ahi, alo):
            s = U % RING
            pe.wait_ge(lo_ready, U + 1)
            if use.n:
                pe.wait_ge(use.freed, use.n)
            wh, wl = wview(whi, s, KT), wview(wlo, s, KT)
            for t in range(NT):
                for k in range(KT):
                    ts = slice(t * P, (t + 1) * P)
                    ins = mm3(pe, use.ps[:, t * T:(t + 1) * T], ahi[:, k, ts], alo[:, k, ts],
                              wh[:, k, :], wl[:, k, :], t == 0 and k == 0, t == 1 and k == KT - 1,
                              t == 0 and k == 0)
            ins.then_inc(use.filled, 1)

        def gemm_rows(pe, U, uses, ahi, alo, first=False, last=False, n=0, i=0):
            s = U % RING
            pe.wait_ge(lo_ready, at_unit(U + 1, n, i))
            wh, wl = wview(whi, s, 2), wview(wlo, s, 2)
            order = [(k, t) for t in range(NT) for k in range(2)] if last else \
                [(k, t) for k in range(2) for t in range(NT)]
            for k, t in order:
                ts = slice(t * P, (t + 1) * P)
                for c in range(2):
                    cs = slice(c * 512, (c + 1) * 512)
                    use = uses[2 * t + c]
                    if first and k == 0 and use.n:
                        pe.wait_ge(use.freed, use.n)
                    ins = mm3(pe, use.ps[:, :], ahi[:, k, ts], alo[:, k, ts], wh[:, k, cs],
                              wl[:, k, cs], first and k == 0, last and k == 1,
                              k == 0 and t == 0 and c == 0)
                    if last and k == 1:
                        ins.then_inc(use.filled, 1)

        nss, nms, nrs = sb("nss", [P, 24]), sb("nms", [P, 24]), sb("nrs", [P, 24])
        mhalf = sb("mhalf", [P, 32])

        groups = [
            [A["dn_conv_w"][0].rearrange("j (k p) -> (j k) p", p=P), A["b_gate_2"][0].rearrange("(k p) -> k p", p=P)],
            [A["ffn_dw_2"][0].rearrange("j (k p) -> (j k) p", p=P)[0:128, :]],
            [A["ffn_dw_2"][0].rearrange("j (k p) -> (j k) p", p=P)[128:132, :],
             A["ffn_dw_b_2"][0].rearrange("(k p) -> k p", p=P), A["b_glu_2"][0].rearrange("(k p) -> k p", p=P),
             A["conv_dw_b_2"][0].rearrange("(k p) -> k p", p=P), A["conv_ln_g_2"][0].rearrange("(k p) -> k p", p=P),
             A["conv_ln_b_2"][0].rearrange("(k p) -> k p", p=P), A["sc_w_2"][0].rearrange("j (k p) -> (j k) p", p=P),
             A["diff_norm_2"], A["dn_out_norm_g"]],
            [A["conv_dw_2"][0].rearrange("j (k p) -> (j k) p", p=P)],
        ]
        g_rows = [sum(x.shape[0] for x in g) for g in groups]
        fc = sb("fc", [P, 4 * P])
        convw = fc[:, 0:96].rearrange("p (j k) -> p j k", j=4)
        b_gate = fc[:, 96:128]
        ffn_w = fc[:, 128:260].rearrange("p (j k) -> p j k", j=3)
        ffn_b, b_glu, dw_b, ln_g, ln_b = fc[:, 260:304], fc[:, 304:312], fc[:, 312:316], fc[:, 316:320], fc[:, 320:324]
        sc_w = fc[:, 324:336].rearrange("p (j k) -> p j k", j=3)
        diff_g, dn_gn = fc[:, 336:337], fc[:, 337:338]
        dw_w = fc[:, 384:508].rearrange("p (j k) -> p j k", j=31)
        sml_rows = sb("sml_rows", [P, 288])
        lam_in = sml_rows[:, 0:256]
        bfgt, alog, dtb = sml_rows[:, 256:264], sml_rows[:, 264:272], sml_rows[:, 272:280]
        small = [
            (alog, A["dn_a_log"].broadcast_to((P, 8))),
            (dtb, A["dn_dt_bias"].broadcast_to((P, 8))),
            (bfgt, A["b_fgt_2"].broadcast_to((P, 8))),
            (lam_in[:, 0:64], A["lam_q1_2"].broadcast_to((P, 64))),
            (lam_in[:, 64:128], A["lam_k1_2"].broadcast_to((P, 64))),
            (lam_in[:, 128:192], A["lam_q2_2"].broadcast_to((P, 64))),
            (lam_in[:, 192:256], A["lam_k2_2"].broadcast_to((P, 64))),
        ]
        stage_rows = common[:, 6144:6656].rearrange("p (g n) -> p g n", g=4)
        for g_, group in enumerate(groups):
            r_ = 0
            for src_ in group:
                small.append((stage_rows[r_:r_ + src_.shape[0], g_, :], src_))
                r_ += src_.shape[0]
        x_in, ba_in, fg_in = sem("x_in"), sem("ba_in"), sem("fg_in")
        N_SMALL = len(small)

        def smalls_loaded(eng):
            eng.wait_ge(const_in, 16 * N_SMALL)

        def constants_built(eng):
            eng.wait_ge(consts_built, 1)

        trio = [common[:, 1536 * p_:1536 * (p_ + 1)] for p_ in range(2)]
        lanes = [common[:, 3072 + 384 * x:3072 + 384 * (x + 1)] for x in range(4)]
        conv_u = common[:, 4608:4608 + 4 * 286].rearrange("p (f t) -> p f t", f=4)
        conv_y = common[:, 5752:5752 + 1024].rearrange("p (f t) -> p f t", f=4)
        diag_f = common[:, 6776:6776 + 1024].rearrange("p (b t) -> p b t", b=8)
        xk = common[:, 7800:7800 + 1024].rearrange("p (f t) -> p f t", f=4)
        xv = common[:, 8824:8824 + 1024].rearrange("p (t n) -> p t n", t=2)
        norm_x = common[:, 0:2048].rearrange("p (t n) -> p t n", t=2)
        hid_r = common[:, 2048:3072].rearrange("p (b n) -> p b n", b=2)
        hid_q = common[:, 3072:4096].rearrange("p (b n) -> p b n", b=2)

        gains = []
        gain_marks = []

        def take_gain(ap):
            gains.append(ap)
            return len(gains) - 1

        def load_gain(pool, g):
            if g < len(gains):
                if g >= 2:
                    pool.wait_ge(gain_marks[g - 2].sem, gain_marks[g - 2].value)
                pool.dma_start(gain[:, g % 2, :], gains[g].broadcast_to((P, D))).then_inc(gain_in[g % 2], 16)

        def gain_loaded(eng, g):
            eng.wait_ge(gain_in[g % 2], 16 * (g // 2 + 1))

        def gain_buf(g):
            return gain[:, g % 2, :]

        norm_count = [0]

        class RootMean:

            def __init__(self, kind):
                self.c = 2 * norm_count[0]
                norm_count[0] += 1
                self.ss, self.ms, self.rs = (x.many(NT) for x in kind)

        def dve_mean_square(dve, r, t):
            c = r.c + t
            dve.wait_ge(r.ss[t].sem, r.ss[t].value)
            nc.vector.tensor_scalar(nms[:, c:c + 1], nss[:, c:c + 1], 1.0 / D, EPS, ALU.mult, ALU.add)\
                .then_inc(r.ms[t].sem, 1)

        def pool_root(pool, r, t):
            c = r.c + t
            pool.wait_ge(r.ms[t].sem, r.ms[t].value)
            nc.gpsimd.tensor_tensor(nrs[:, c:c + 1], nms[:, c:c + 1], mhalf[:, 0:1], ALU.pow)\
                .then_inc(r.rs[t].sem, 1)

        def transposed_norm(src, g_ap, src_ready, dst_hi, dst_lo):
            r = RootMean(norm_kinds[0])
            g = take_gain(g_ap)
            xn = xn_ready.many(NT)
            gain_marks.append(xn[1])
            uses = [b.use() for b in G]
            hi = x_hi.many(4)

            def act_tile(act, t):
                c = r.c + t
                act.wait_ge(*src_ready(t))
                nc.scalar.activation(norm_x[:, t, :], src[t], ACT.Square,
                                     accum_out=nss[:, c:c + 1]).then_inc(r.ss[t].sem, 1)

            def dve_after(dve, t):
                dve.wait_ge(r.rs[t].sem, r.rs[t].value)
                gain_loaded(dve, g)
                nc.vector.scalar_tensor_tensor(norm_x[:, t, :], src[t], nrs[:, r.c + t:r.c + t + 1],
                                               gain_buf(g), ALU.mult, ALU.mult).then_inc(xn[t].sem, 1)

            def pe_transposes(pe):
                for q in range(4):
                    t, k0 = q // 2, 4 * (q % 2)
                    pe.wait_ge(xn[t].sem, xn[t].value)
                    if uses[q].n:
                        pe.wait_ge(uses[q].freed, uses[q].n)
                    for k in range(4):
                        ins = pe.transpose(uses[q].ps[:, k * P:(k + 1) * P],
                                           norm_x[:, t, (k0 + k) * P:(k0 + k + 1) * P], ident[:, :])
                    ins.then_inc(uses[q].filled, 1)

            def part(dst, q):
                t, k0 = q // 2, 4 * (q % 2)
                return dst[:, k0:k0 + 4, t * P:(t + 1) * P]

            def ps4(q):
                return uses[q].ps[:, :].rearrange("p (k n) -> p k n", k=4)

            def act_parts(act):
                for q in range(4):
                    act.wait_ge(uses[q].filled, uses[q].n + 1)
                    nc.scalar.activation(part(dst_hi, q), ps4(q), ACT.Copy).then_inc(hi[q].sem, 1)

            def dve_parts(dve):
                for q in range(4):
                    dve.wait_ge(hi[q].sem, hi[q].value)
                    nc.vector.tensor_tensor(part(dst_lo, q), ps4(q), f32(part(dst_hi, q)), ALU.subtract)\
                        .then_inc(uses[q].freed, 1)

            return Norm(act_tile, lambda dve, t: dve_mean_square(dve, r, t), dve_after, lambda pool, t: pool_root(pool, r, t), g,
                        pe=pe_transposes, act_parts=act_parts, dve_parts=dve_parts, parts=uses)

        def wait_parts(pe, norm):
            for use in norm.parts:
                pe.wait_ge(use.freed, use.n + 1)

        def add_rows(uses):
            def dve_tile(dve, t):
                for c in range(2):
                    use = uses[2 * t + c]
                    dve.wait_ge(use.filled, use.n + 1)
                    hs = h[:, t, c * 512:(c + 1) * 512]
                    nc.vector.tensor_tensor(hs, use.ps[:, :], hs, ALU.add).then_inc(use.freed, 1)

            return Norm(None, dve_tile, None, None, None, ready=lambda t: uses[2 * t + 1].done)

        def add_normed_rows(uses, g_ap):
            r = RootMean(norm_kinds[1])
            g = take_gain(g_ap)
            marks = h_ready.many(NT)
            gain_marks.append(marks[1])

            def act_tile(act, t):
                for k in range(2):
                    use = uses[2 * t + k]
                    act.wait_ge(use.filled, use.n + 1)
                    unused = common[:, 2048 + 512 * (2 * t + k):2560 + 512 * (2 * t + k)]
                    ins = nc.scalar.activation(unused, use.ps[:, :], ACT.Square,
                                               accum_out=psum_ss[:, 2 * t + k:2 * t + k + 1])
                ins.then_inc(r.ss[t].sem, 1)

            def dve_before(dve, t):
                dve.wait_ge(r.ss[t].sem, r.ss[t].value)
                c = r.c + t
                nc.vector.tensor_tensor(nss[:, c:c + 1], psum_ss[:, 2 * t:2 * t + 1],
                                        psum_ss[:, 2 * t + 1:2 * t + 2], ALU.add)\
                    .then_inc(dve_self.sem, dve_self.add(1))
                dve.wait_ge(dve_self.sem, dve_self.n)
                dve_mean_square(dve, r, t)
                gain_loaded(dve, g)
                for k in range(2):
                    use, ks = uses[2 * t + k], slice(k * 512, (k + 1) * 512)
                    dve.wait_ge(use.filled, use.n + 1)
                    nc.vector.tensor_tensor(norm_x[:, t, ks], use.ps[:, :], gain_buf(g)[:, ks], ALU.mult)\
                        .then_inc(use.freed, 1)

            def dve_after(dve, t):
                for use in uses[2 * t:2 * t + 2]:
                    dve.wait_ge(use.freed, use.n + 1)
                dve.wait_ge(r.rs[t].sem, r.rs[t].value)
                nc.vector.scalar_tensor_tensor(h[:, t, :], norm_x[:, t, :], nrs[:, r.c + t:r.c + t + 1], h[:, t, :],
                                               ALU.mult, ALU.add).then_inc(marks[t].sem, 1)

            return Norm(act_tile, dve_before, dve_after, lambda pool, t: pool_root(pool, r, t), g,
                        ready=lambda t: marks[t].done)

        def norm_in_place(src_ready, g_ap):
            r = RootMean(norm_kinds[2])
            g = take_gain(g_ap)
            marks = h_ready.many(NT)
            gain_marks.append(marks[1])

            def act_tile(act, t):
                c = r.c + t
                act.wait_ge(*src_ready(t))
                nc.scalar.activation(norm_x[:, t, :], h[:, t, :], ACT.Square,
                                     accum_out=nss[:, c:c + 1]).then_inc(r.ss[t].sem, 1)

            def dve_after(dve, t):
                dve.wait_ge(r.rs[t].sem, r.rs[t].value)
                gain_loaded(dve, g)
                nc.vector.scalar_tensor_tensor(h[:, t, :], h[:, t, :], nrs[:, r.c + t:r.c + t + 1], gain_buf(g),
                                               ALU.mult, ALU.mult).then_inc(marks[t].sem, 1)

            return Norm(act_tile, lambda dve, t: dve_mean_square(dve, r, t), dve_after, lambda pool, t: pool_root(pool, r, t), g,
                        ready=lambda t: marks[t].done)

        def act_tiles(act, *chain):
            for t in range(NT):
                for n in chain:
                    n.act_tile(act, t)

        def act_tiles_of_two(act, product, turned):
            for n in (product, turned):
                for t in range(NT):
                    n.act_tile(act, t)

        def dve_tiles(dve, *chain):
            for t in range(NT):
                for n in chain:
                    n.dve_before(dve, t)
                    if n.dve_after:
                        n.dve_after(dve, t)

        def dve_tiles_of_two(dve, product, turned):
            product.dve_before(dve, 0)
            product.dve_after(dve, 0)
            product.dve_before(dve, 1)
            turned.dve_before(dve, 0)
            product.dve_after(dve, 1)
            turned.dve_after(dve, 0)
            turned.dve_before(dve, 1)
            turned.dve_after(dve, 1)

        def pool_tiles(pool, *chain):
            for t in range(NT):
                for n in chain:
                    n.pool_tile(pool, t)
            for n in chain:
                load_gain(pool, n.g + 2)

        def mlp(up, down, norm):
            NB = 4 * D // 256
            a0, a1 = unit(features(up, 0)), unit(features(up, 256))
            d0 = unit(rows(down, 0))
            loop = (NB - 2) // 2
            L = unit_loop(loop, [lambda i: features(up, 512 + 512 * i), lambda i: rows(down, 256 + 512 * i),
                                 lambda i: features(up, 768 + 512 * i), lambda i: rows(down, 512 + 512 * i)])
            dl = unit(rows(down, (NB - 1) * 256))
            ua = [G[0].use(), G[1].use()]
            hi_s, f_s, lo_s = (x.many(2) for x in (hid_sq, hid_f32, hid_lo))
            ul = [G[0].loop(loop, 1)[0], G[1].loop(loop, 1)[0]]
            hi_l, f_l, lo_l = (x.loop(loop, 2) for x in (hid_sq, hid_f32, hid_lo))
            acc = [b.use() for b in O]

            def act_a(act, U, p_, use, hi_, n=0, i=0):
                split_hi(act, U, n, i)
                act.wait_ge(use.filled, use.at(i) + 1)
                nc.scalar.activation(hid_r[:, p_, :], use.ps[:, :], ACT.Relu).then_inc(use.freed, 1)
                act.wait_ge(use.freed, use.at(i) + 1)
                nc.scalar.activation(hhi[:, p_].rearrange("p k n -> p (k n)"), hid_r[:, p_, :],
                                                ACT.Square).then_inc(hi_.sem, 1)

            def dve_a(dve, U, p_, use, hi_, f_, lo_, n=0, i=0):
                split_lo(dve, U, n, i)
                dve.wait_ge(use.freed, use.at(i) + 1)
                nc.vector.tensor_tensor(hid_q[:, p_, :], hid_r[:, p_, :], hid_r[:, p_, :], ALU.mult)\
                    .then_inc(f_.sem, 1)
                dve.wait_ge(f_.sem, f_.at(i))
                dve.wait_ge(hi_.sem, hi_.at(i))
                nc.vector.tensor_tensor(hlo[:, p_].rearrange("p k n -> p (k n)"), hid_q[:, p_, :],
                                                   f32(hhi[:, p_].rearrange("p k n -> p (k n)")), ALU.subtract)\
                                                       .then_inc(lo_.sem, 1)

            def pe_f(pe):
                wait_parts(pe, norm)
                gemm_features(pe, a0, ua[0], xhi, xlo)
                gemm_features(pe, a1, ua[1], xhi, xlo)
                pe.wait_ge(lo_s[0].sem, lo_s[0].value)
                gemm_rows(pe, d0, acc, hhi[:, 0], hlo[:, 0], first=True)
                with pe.Fori(0, loop) as i:
                    gemm_features(pe, L[0], ul[0], xhi, xlo, 4, i)
                    pe.wait_ge(hid_lo.sem, lo_s[1].value + 2 * i)
                    gemm_rows(pe, L[1], acc, hhi[:, 1], hlo[:, 1], n=4, i=i)
                    gemm_features(pe, L[2], ul[1], xhi, xlo, 4, i)
                    pe.wait_ge(lo_l[0].sem, lo_l[0].at(i))
                    gemm_rows(pe, L[3], acc, hhi[:, 0], hlo[:, 0], n=4, i=i)
                pe.wait_ge(hid_lo.sem, lo_s[1].value + 2 * loop)
                gemm_rows(pe, dl, acc, hhi[:, 1], hlo[:, 1], last=True)

            def act_f(act):
                act_a(act, a0, 0, ua[0], hi_s[0])
                act_a(act, a1, 1, ua[1], hi_s[1])
                split_hi(act, d0)
                with act.Fori(0, loop) as i:
                    act_a(act, L[0], 0, ul[0], hi_l[0], 4, i)
                    split_hi(act, L[1], 4, i)
                    act_a(act, L[2], 1, ul[1], hi_l[1], 4, i)
                    split_hi(act, L[3], 4, i)
                split_hi(act, dl)

            def dve_f(dve):
                dve_a(dve, a0, 0, ua[0], hi_s[0], f_s[0], lo_s[0])
                dve_a(dve, a1, 1, ua[1], hi_s[1], f_s[1], lo_s[1])
                split_lo(dve, d0)
                with dve.Fori(0, loop) as i:
                    dve_a(dve, L[0], 0, ul[0], hi_l[0], f_l[0], lo_l[0], 4, i)
                    split_lo(dve, L[1], 4, i)
                    dve_a(dve, L[2], 1, ul[1], hi_l[1], f_l[1], lo_l[1], 4, i)
                    split_lo(dve, L[3], 4, i)
                split_lo(dve, dl)

            return Part(pe=pe_f, act=act_f, dve=dve_f, acc=acc)

        HN = 8
        qkv = extra[:, 96:96 + 6144].rearrange("p (f t) -> p f t", f=24)
        zt = common[:, 0:2048].rearrange("p (f t) -> p f t", f=8)
        sq = common[:, 2048:6144].rearrange("p (f t) -> p f t", f=16)
        dk = common[:, 2048:3072].rearrange("p (t h n) -> p t h n", t=2, h=4)
        dgu = common[:, 3072:4096].rearrange("p (t h n) -> p t h n", t=2, h=4)
        dgb = common[:, 4096:5120].rearrange("p (t h n) -> p t h n", t=2, h=4)
        yb = common[:, 5120:6144].rearrange("p (t h n) -> p t h n", t=2, h=4)
        bm = common[:, 6144:7168].rearrange("p (t h n) -> p t h n", t=2, h=4)
        xi = common[:, 7168:8192].rearrange("p (t h n) -> p t h n", t=2, h=4)
        xt = common[:, 8192:9216].rearrange("p (t h n) -> p t h n", t=2, h=4)
        at = extra[:, 6240:7264].rearrange("p (t h n) -> p t h n", t=2, h=4)
        vb = [v.rearrange("p (h n) -> p h n", h=4) for v in (masks[:, 0:512], common[:, 9216:9728])]
        kd, st = xi[:, 0], xi[:, 1]
        levels = extra[:, 7264:7264 + 7 * 128].rearrange("p (l n) -> p l n", l=7)
        lowerk = dn_lower[:, :]
        ba = sm[:, 0:32].rearrange("p (t n) -> p t n", t=2)
        beta, gg, gcum, egc = (sm[:, 32 + 16 * j:48 + 16 * j].rearrange("p (t n) -> p t n", t=2) for j in range(4))
        rsq = sm[:, 96:128]
        rq, rk = (rsq[:, 16 * j:16 * j + 16].rearrange("p (t n) -> p t n", t=2) for j in range(2))
        tmp = [sm[:, 128 + 16 * j:144 + 16 * j].rearrange("p (t n) -> p t n", t=2) for j in range(5)]
        nbk, nbek, kdec = (sm[:, 208 + 16 * j:224 + 16 * j].rearrange("p (t n) -> p t n", t=2) for j in range(3))
        sso, fo = (smo[:, 16 * j:16 * j + 16].rearrange("p (t n) -> p t n", t=2) for j in range(2))
        msn = smo[:, 32:64]

        def deltanet_in(norm):
            W = A["dn_w_in"][0]
            units = [unit(features(W, 256 * u)) for u in range(12)]
            uses = [G[u % 4].use() for u in range(12)]
            uba = O[0].use()
            first_tap, silus, squares = a2d.many(12), a2p.many(12), p2t.many(8)
            uss = O[1].use()

            def pe_in(pe):
                wait_parts(pe, norm)
                pe.wait_ge(sm_lo.sem, sm_lo.value)
                for t in range(NT):
                    for k in range(KT):
                        ts = slice(t * P, (t + 1) * P)
                        ins = mm3(pe, uba.ps[:, 16 * t:16 * t + 16], xhi[:, k, ts], xlo[:, k, ts],
                                  smh[:, k, :], sml[:, k, :], t == 0 and k == 0, t == 1 and k == KT - 1)
                ins.then_inc(uba.filled, 1)
                for u in range(12):
                    gemm_features(pe, units[u], uses[u], xhi, xlo)

            def finish_unit(act, u):
                act.wait_ge(uses[u].freed, uses[u].n + 1)
                nc.scalar.activation(qkv[:, 2 * u:2 * u + 2, :], qkv[:, 2 * u:2 * u + 2, :],
                                                     ACT.Silu).then_inc(silus[u].sem, 1)

            def act_in(act):
                for u in range(12):
                    split_hi(act, units[u])
                    if u:
                        finish_unit(act, u - 1)
                    act.wait_ge(uses[u].filled, uses[u].n + 1)
                    for f in range(2):
                        ft = 2 * u + f
                        ins = nc.scalar.activation(qkv[:, ft, :], uses[u].ps[:, f * T:(f + 1) * T], ACT.Copy,
                                                   scale=convw[:, 3, ft:ft + 1])
                    ins.then_inc(first_tap[u].sem, 1)
                finish_unit(act, 11)

            def dve_in(dve):
                for u in range(12):
                    split_lo(dve, units[u])
                    dve.wait_ge(first_tap[u].sem, first_tap[u].value)
                    for j in (2, 1, 0):
                        for f in range(2):
                            ft = 2 * u + f
                            sh = 3 - j
                            if j < 2:
                                dve.wait_ge(dve_self.sem, dve_self.n - 1)
                            ins = nc.vector.scalar_tensor_tensor(
                                qkv[:, ft, sh:T], uses[u].ps[:, f * T:(f + 1) * T - sh],
                                convw[:, j, ft:ft + 1], qkv[:, ft, sh:T], ALU.mult, ALU.add)
                            if j == 0 and f == 1:
                                ins.then_inc(uses[u].freed, 1)
                            else:
                                ins.then_inc(dve_self.sem, dve_self.add(1))

            def pool_in(pool):
                for u in range(8):
                    pool.wait_ge(silus[u].sem, silus[u].value)
                    s2 = slice(2 * u, 2 * u + 2)
                    nc.gpsimd.tensor_tensor(sq[:, s2, :], qkv[:, s2, :], qkv[:, s2, :], ALU.mult)\
                        .then_inc(squares[u].sem, 1)

            return Part(pe=pe_in, act=act_in, dve=dve_in, pool=pool_in, uba=uba, uss=uss, squares=squares)

        def z_block(j, bank):
            return block_of(A["dn_w_in"][0], 3 * D + 256 * j, bank)

        def act_z(act, b, j, func):
            act.wait_ge(b.use.filled, b.use.n + 1)
            nc.scalar.activation(zt[:, 2 * j:2 * j + 2, :], two(b.use.ps[:, :]), func).then_inc(b.use.freed, 1)

        def deltanet_scalars(proj):
            z = z_block(0, G[0])
            uba, uss, squares = proj.uba, proj.uss, proj.squares
            roots = p2d.next()
            al, e1, e2, l1 = a2d.many(4)
            z_d, u_d = d2a.next(), d2a.next()
            g_d = d2t.next()
            ugc, ugl = O[2].use(), O[3].use()
            gc_a, kl_a = a2d.next(), a2d.next()

            def pe_s(pe):
                pe.wait_ge(squares[7].sem, squares[7].value)
                if uss.n:
                    pe.wait_ge(uss.freed, uss.n)
                for x in range(2):
                    for t in range(NT):
                        for hd in range(HN):
                            c = 16 * x + 8 * t + hd
                            ins = pe.matmul(uss.ps[:, c:c + 1], sq[:, 8 * x + hd, t * P:(t + 1) * P],
                                            ones[:, 0:1], start=(c == 0), stop=(c == 31),
                                            skip_group_check=True)
                ins.then_inc(uss.filled, 1)
                block_product(pe, z)
                pe.wait_ge(g_d.sem, g_d.value)
                if ugc.n:
                    pe.wait_ge(ugc.freed, ugc.n)
                pe.matmul(ugc.ps[:, 0:16], upper[:, :], sm[:, 48:64], start=True, stop=True)\
                    .then_inc(ugc.filled, 1)
                if ugl.n:
                    pe.wait_ge(ugl.freed, ugl.n)
                pe.matmul(ugl.ps[:, 0:8], ones[:, :], sm[:, 48:56], start=True, stop=True)\
                    .then_inc(ugl.filled, 1)

            def act_s(act):
                smalls_loaded(act)
                nc.scalar.activation(alog, alog, ACT.Exp).then_inc(al.sem, 1)
                act.wait_ge(uba.freed, uba.n + 1)
                nc.scalar.activation(tmp[0], ba[:, :, 0:8], ACT.Exp, scale=-1.0).then_inc(e1.sem, 1)
                act.wait_ge(z_d.sem, z_d.value)
                nc.scalar.activation(tmp[2], tmp[2], ACT.Exp, scale=-1.0).then_inc(e2.sem, 1)
                act.wait_ge(u_d.sem, u_d.value)
                nc.scalar.activation(tmp[4], tmp[3], ACT.Ln).then_inc(l1.sem, 1)
                act.wait_ge(ugc.filled, ugc.n + 1)
                nc.scalar.activation(egc, ugc.ps[:, 0:16].rearrange("p (t n) -> p t n", t=2), ACT.Exp)\
                    .then_inc(gc_a.sem, 1)
                act.wait_ge(ugl.freed, ugl.n + 1)
                nc.scalar.activation(kdec[:, 0, :], kdec[:, 0, :], ACT.Exp).then_inc(kl_a.sem, 1)
                act_z(act, z, 0, ACT.Copy)
                split_hi(act, z.U)

            def dve_s(dve):
                dc = dve_self

                def link(ins):
                    ins.then_inc(dc.sem, dc.add(1))
                    dve.wait_ge(dc.sem, dc.n)

                dve.wait_ge(uba.filled, uba.n + 1)
                nc.vector.tensor_copy(sm[:, 0:32], uba.ps[:, 0:32]).then_inc(uba.freed, 1)
                dve.wait_ge(uba.freed, uba.n + 1)
                dve.wait_ge(al.sem, al.value)
                link(nc.vector.tensor_tensor(tmp[1], ba[:, :, 8:16], bc3(dtb, 2), ALU.add))
                link(nc.vector.tensor_scalar(tmp[2], tmp[1], -1.0, None, ALU.mult))
                link(nc.vector.tensor_tensor(tmp[2], tmp[2], tmp[1], ALU.max))
                nc.vector.tensor_scalar(tmp[1], tmp[1], 0.0, None, ALU.max).then_inc(z_d.sem, 1)
                dve.wait_ge(e1.sem, e1.value)
                link(nc.vector.tensor_scalar(tmp[0], tmp[0], 1.0, None, ALU.add))
                link(nc.vector.reciprocal(beta, tmp[0]))
                dve.wait_ge(e2.sem, e2.value)
                link(nc.vector.tensor_scalar(tmp[3], tmp[2], 1.0, None, ALU.add))
                nc.vector.tensor_scalar(tmp[0], tmp[3], -1.0, None, ALU.add).then_inc(u_d.sem, 1)
                dve.wait_ge(u_d.sem, u_d.value)
                link(nc.vector.tensor_tensor(tmp[2], tmp[2], tmp[0], ALU.subtract))
                link(nc.vector.tensor_tensor(tmp[1], tmp[1], tmp[2], ALU.add))
                dve.wait_ge(l1.sem, l1.value)
                link(nc.vector.tensor_tensor(tmp[1], tmp[1], tmp[4], ALU.add))
                link(nc.vector.tensor_tensor(tmp[1], tmp[1], bc3(alog, 2), ALU.mult))
                nc.vector.tensor_scalar(gg, tmp[1], -1.0, None, ALU.mult).then_inc(g_d.sem, 1)
                dve.wait_ge(uss.filled, uss.n + 1)
                nc.vector.tensor_scalar(msn, uss.ps[:, 0:32], EPS, None, ALU.add).then_inc(uss.freed, 1)
                dve.wait_ge(roots.sem, roots.value)
                link(nc.vector.tensor_scalar(rsq[:, 0:16], rsq[:, 0:16], 128.0 ** -0.5, None, ALU.mult))
                link(nc.vector.scalar_tensor_tensor(nbk, beta, -1.0, rk, ALU.mult, ALU.mult))
                dve.wait_ge(ugc.filled, ugc.n + 1)
                dve.wait_ge(gc_a.sem, gc_a.value)
                nc.vector.tensor_copy(gcum, ugc.ps[:, 0:16].rearrange("p (t n) -> p t n", t=2))\
                    .then_inc(ugc.freed, 1)
                dve.wait_ge(ugc.freed, ugc.n + 1)
                link(nc.vector.tensor_tensor(nbek, nbk, egc, ALU.mult))
                dve.wait_ge(ugl.filled, ugl.n + 1)
                nc.vector.tensor_tensor(kdec[:, 0, :], ugl.ps[:, 0:8], gcum[:, 0, :], ALU.subtract)\
                    .then_inc(ugl.freed, 1)
                dve.wait_ge(kl_a.sem, kl_a.value)
                link(nc.vector.tensor_tensor(kdec[:, 0, :], kdec[:, 0, :], rk[:, 0, :], ALU.mult))

            def pool_s(pool):
                pool.wait_ge(uss.freed, uss.n + 1)
                nc.gpsimd.tensor_tensor(rsq, msn, mhalf[:, :], ALU.pow).then_inc(roots.sem, 1)

            return Part(pe=pe_s, act=act_s, dve=dve_s, pool=pool_s, last=z)

        def deltanet_group(grp, z0, before=None):
            H0 = 4 * grp
            bs = [[G[2 * t], G[2 * t + 1], O[2 * t], O[2 * t + 1]] for t in range(NT)]
            diags = d2t.many(NT)
            uD = [bs[t][0].use() for t in range(NT)]
            uG = [bs[t][1].use() for t in range(NT)]
            uKQ = [bs[t][2].use() for t in range(NT)]
            uRB = [bs[t][3].use() for t in range(NT)]
            b_done = [d2t.next() for _ in range(NT)]
            b_free = [p2d.next() for _ in range(NT)]
            uT = [bs[t][2].use() for t in range(NT)]
            lv = []
            for s in range(1, 7):
                lv.append([(bs[t][0].use(), bs[t][1].use(), bs[t][2].use() if s < 6 else None) for t in range(NT)])
            uV = [bs[t][3].use() for t in range(NT)]
            uK = bs[0][2].use()
            uU0, uO0, uS = bs[0][0].use(), bs[0][1].use(), bs[0][3].use()
            uKS, uQS, uU1, uO1 = bs[1][0].use(), bs[1][1].use(), bs[1][2].use(), bs[1][3].use()
            z1 = z_block(2 * grp + 1, bs[0][2])
            z_silu = a2d.next()
            o_ss, o_ms, o_rt = a2d.next(), d2p.next(), p2d.next()
            on_d = d2t.many(2)
            uY = [bs[0][0].use(), bs[0][1].use()]
            z2 = None if grp else z_block(2, bs[0][2])
            y_hi, y_lo = a2d.many(2), d2t.many(2)

            def blk(use, hd):
                return use.ps[:, hd * P:(hd + 1) * P]

            def flat(ap):
                return ap.rearrange("p h n -> p (h n)")

            def kt_(hd, t):
                return qkv[:, 8 + H0 + hd, t * P:(t + 1) * P]

            def qt_(hd, t):
                return qkv[:, H0 + hd, t * P:(t + 1) * P]

            def four(pe, use, lhs, rhs):
                if use.n:
                    pe.wait_ge(use.freed, use.n)
                for hd in range(4):
                    ins = pe.matmul(blk(use, hd), lhs(hd), rhs(hd), start=(hd == 0), stop=(hd == 3),
                                    skip_group_check=True)
                ins.then_inc(use.filled, 1)

            def pe_f(pe):
                for t in range(NT):
                    pe.wait_ge(diags[t].sem, diags[t].value)
                    if uD[t].n:
                        pe.wait_ge(uD[t].freed, uD[t].n)
                    pe.matmul(uD[t].ps[:, :], lowerk, flat(dgu[:, t]), start=True, stop=True)\
                        .then_inc(uD[t].filled, 1)
                    if uRB[t].n:
                        pe.wait_ge(uRB[t].freed, uRB[t].n)
                    pe.matmul(uRB[t].ps[:, :], ones[:, :], flat(dgb[:, t]), start=True, stop=True)\
                        .then_inc(uRB[t].filled, 1)
                    four(pe, uG[t], lambda hd: kt_(hd, t), lambda hd: kt_(hd, t))
                    four(pe, uKQ[t], lambda hd: kt_(hd, t), lambda hd: qt_(hd, t))
                for t in range(NT):
                    pe.wait_ge(b_done[t].sem, b_done[t].value)
                    if uT[t].n:
                        pe.wait_ge(uT[t].freed, uT[t].n)
                    for hd in range(4):
                        ins = pe.transpose(blk(uT[t], hd), xt[:, t, hd, :], ident[:, :])
                    ins.then_inc(uT[t].filled, 1)
                for s in range(6):
                    for t in range(NT):
                        use = lv[s - 1][t][2] if s else uT[t]
                        pe.wait_ge(use.freed, use.n + 1)
                        four(pe, lv[s][t][0], lambda hd: bm[:, t, hd, :], lambda hd: xi[:, t, hd, :])
                    for t in range(NT):
                        pe.wait_ge(lv[s][t][0].freed, lv[s][t][0].n + 1)
                        four(pe, lv[s][t][1], lambda hd: yb[:, t, hd, :], lambda hd: xt[:, t, hd, :])
                    for t in range(NT):
                        pe.wait_ge(lv[s][t][1].freed, lv[s][t][1].n + 1)
                        if s < 5:
                            use = lv[s][t][2]
                            if use.n:
                                pe.wait_ge(use.freed, use.n)
                            for hd in range(4):
                                ins = pe.transpose(blk(use, hd), xt[:, t, hd, :], ident[:, :])
                            ins.then_inc(use.filled, 1)
                    if s == 0:
                        for t in range(NT):
                            if uV[t].n:
                                pe.wait_ge(uV[t].freed, uV[t].n)
                            for hd in range(4):
                                ins = pe.transpose(blk(uV[t], hd), qkv[:, 16 + H0 + hd, t * P:(t + 1) * P],
                                                   ident[:, :])
                            ins.then_inc(uV[t].filled, 1)
                if uK.n:
                    pe.wait_ge(uK.freed, uK.n)
                for hd in range(4):
                    ins = pe.transpose(blk(uK, hd), kt_(hd, 0), ident[:, :])
                ins.then_inc(uK.filled, 1)
                pe.wait_ge(uV[0].freed, uV[0].n + 1)
                four(pe, uU0, lambda hd: xt[:, 0, hd, :], lambda hd: vb[0][:, hd, :])
                pe.wait_ge(uU0.freed, uU0.n + 1)
                pe.wait_ge(uK.freed, uK.n + 1)
                four(pe, uS, lambda hd: kd[:, hd, :], lambda hd: dgu[:, 0, hd, :])
                four(pe, uO0, lambda hd: at[:, 0, hd, :], lambda hd: dgu[:, 0, hd, :])
                features_part(pe, z1.U, z1.use, xhi, xlo, 0, 2)
                pe.wait_ge(uS.freed, uS.n + 1)
                four(pe, uKS, lambda hd: kt_(hd, 1), lambda hd: st[:, hd, :])
                four(pe, uQS, lambda hd: qt_(hd, 1), lambda hd: st[:, hd, :])
                features_part(pe, z1.U, z1.use, xhi, xlo, 2, 4)
                pe.wait_ge(uKS.freed, uKS.n + 1)
                four(pe, uU1, lambda hd: xt[:, 1, hd, :], lambda hd: vb[1][:, hd, :])
                features_part(pe, z1.U, z1.use, xhi, xlo, 4, 7)
                pe.wait_ge(uU1.freed, uU1.n + 1)
                four(pe, uO1, lambda hd: at[:, 1, hd, :], lambda hd: dgu[:, 1, hd, :])
                features_part(pe, z1.U, z1.use, xhi, xlo, 7, 2 * KT)
                for pr in range(2):
                    pe.wait_ge(on_d[pr].sem, on_d[pr].value)
                    if uY[pr].n:
                        pe.wait_ge(uY[pr].freed, uY[pr].n)
                    for e in range(2):
                        for t in range(NT):
                            ins = pe.transpose(uY[pr].ps[:, e * T + t * P:e * T + (t + 1) * P],
                                               dgb[:, t, 2 * pr + e, :], ident[:, :])
                    ins.then_inc(uY[pr].filled, 1)
                if z2:
                    block_product(pe, z2)

            def act_f(act):
                for t in range(NT):
                    act.wait_ge(uD[t].filled, uD[t].n + 1)
                    nc.scalar.activation(flat(dk[:, t]), uD[t].ps[:, :], ACT.Exp).then_inc(uD[t].freed, 1)
                for t in range(NT):
                    act.wait_ge(uT[t].filled, uT[t].n + 1)
                    nc.scalar.activation(flat(xi[:, t]), uT[t].ps[:, :], ACT.Copy).then_inc(uT[t].freed, 1)
                for s in range(6):
                    for t in range(NT):
                        use = lv[s][t][0]
                        act.wait_ge(use.filled, use.n + 1)
                        nc.scalar.activation(flat(yb[:, t]), use.ps[:, :], ACT.Copy).then_inc(use.freed, 1)
                    if s < 5:
                        for t in range(NT):
                            use = lv[s][t][2]
                            act.wait_ge(use.filled, use.n + 1)
                            nc.scalar.activation(flat(xi[:, t]), use.ps[:, :], ACT.Copy).then_inc(use.freed, 1)
                    if s == 0:
                        for t in range(NT):
                            act.wait_ge(uV[t].filled, uV[t].n + 1)
                            for hd in range(4):
                                ins = nc.scalar.activation(vb[t][:, hd, :], blk(uV[t], hd), ACT.Copy,
                                                           scale=beta[:, t, H0 + hd:H0 + hd + 1])
                            ins.then_inc(uV[t].freed, 1)
                    if s == 1:
                        act.wait_ge(z0.use.freed, z0.use.n + 1)
                        nc.scalar.activation(zt[:, H0:H0 + 2, :], zt[:, H0:H0 + 2, :], ACT.Silu)\
                            .then_inc(z_silu.sem, 1)
                act.wait_ge(uK.filled, uK.n + 1)
                for hd in range(4):
                    ins = nc.scalar.activation(kd[:, hd, :], blk(uK, hd), ACT.Copy,
                                               scale=kdec[:, 0, H0 + hd:H0 + hd + 1])
                ins.then_inc(uK.freed, 1)
                act.wait_ge(uU0.filled, uU0.n + 1)
                nc.scalar.activation(flat(dgu[:, 0]), uU0.ps[:, :], ACT.Copy).then_inc(uU0.freed, 1)
                act.wait_ge(uS.filled, uS.n + 1)
                nc.scalar.activation(flat(st), uS.ps[:, :], ACT.Copy).then_inc(uS.freed, 1)
                act.wait_ge(uO0.filled, uO0.n + 1)
                nc.scalar.activation(flat(dgb[:, 0]), uO0.ps[:, :], ACT.Copy).then_inc(uO0.freed, 1)
                split_hi(act, z1.U)
                act.wait_ge(uQS.filled, uQS.n + 1)
                for hd in range(4):
                    ins = nc.scalar.activation(yb[:, 0, hd, :], blk(uQS, hd), ACT.Copy,
                                               scale=egc[:, 1, H0 + hd:H0 + hd + 1])
                ins.then_inc(uQS.freed, 1)
                act.wait_ge(uU1.filled, uU1.n + 1)
                nc.scalar.activation(flat(dgu[:, 1]), uU1.ps[:, :], ACT.Copy).then_inc(uU1.freed, 1)
                act.wait_ge(uO0.freed, uO0.n + 1)
                for t in range(NT):
                    if t == 1:
                        act.wait_ge(uO1.freed, uO1.n + 1)
                    for hd in range(4):
                        ins = nc.scalar.activation(dk[:, t, hd, :], dgb[:, t, hd, :], ACT.Square,
                                                   scale=rq[:, t, H0 + hd:H0 + hd + 1],
                                                   accum_out=sso[:, t, H0 + hd:H0 + hd + 1])
                ins.then_inc(o_ss.sem, 1)
                act_z(act, z1, 2 * grp + 1, ACT.Silu)
                for pr in range(2):
                    act.wait_ge(uY[pr].freed, uY[pr].n + 1)
                    nc.scalar.activation(y_parts[pr][0], ytmp(pr), ACT.Copy).then_inc(y_hi[pr].sem, 1)
                if z2:
                    split_hi(act, z2.U)
                    act_z(act, z2, 2, ACT.Copy)

            y_parts = [(xhi[:, 2 * pr:2 * pr + 2, :], xlo[:, 2 * pr:2 * pr + 2, :]) if grp else
                       (hhi[:, pr], hlo[:, pr]) for pr in range(2)]

            def ytmp(pr):
                return flat(xi[:, pr]).rearrange("p (f t) -> p f t", f=2)

            def dve_f(dve):
                for t in range(NT):
                    for hd in range(4):
                        nc.vector.tensor_scalar(dgu[:, t, hd, :], upper[:, :],
                                                gg[:, t, H0 + hd:H0 + hd + 1], None, ALU.mult)
                        ins = nc.vector.tensor_scalar(dgb[:, t, hd, :], ident[:, :],
                                                      nbk[:, t, H0 + hd:H0 + hd + 1], None, ALU.mult)
                    ins.then_inc(diags[t].sem, 1)
                split_lo(dve, z0.U)
                for t in range(NT):
                    dve.wait_ge(uD[t].freed, uD[t].n + 1)
                    for hd in range(4):
                        nc.vector.scalar_tensor_tensor(
                            dk[:, t, hd, :], dk[:, t, hd, :], rk[:, t, H0 + hd:H0 + hd + 1], upper[:, :],
                            ALU.mult, ALU.mult).then_inc(dve_self.sem, dve_self.add(1))
                    dve.wait_ge(dve_self.sem, dve_self.n)
                    dve.wait_ge(uKQ[t].filled, uKQ[t].n + 1)
                    nc.vector.tensor_tensor(flat(at[:, t]), uKQ[t].ps[:, :], flat(dk[:, t]), ALU.mult)\
                        .then_inc(uKQ[t].freed, 1)
                    dve.wait_ge(uG[t].filled, uG[t].n + 1)
                    nc.vector.tensor_tensor(flat(bm[:, t]), uG[t].ps[:, :], flat(dk[:, t]), ALU.mult)\
                        .then_inc(uG[t].freed, 1)
                    dve.wait_ge(uG[t].freed, uG[t].n + 1)
                    dve.wait_ge(uRB[t].filled, uRB[t].n + 1)
                    nc.vector.tensor_tensor(flat(bm[:, t]), uRB[t].ps[:, :], flat(bm[:, t]), ALU.mult)\
                        .then_inc(uRB[t].freed, 1)
                    dve.wait_ge(uRB[t].freed, uRB[t].n + 1)
                    dve.wait_ge(b_free[t].sem, b_free[t].value)
                    nc.vector.copy_predicated(xt[:, t], bc3(levels[:, 0, :].bitcast(I32), 4),
                                                               bm[:, t]).then_inc(b_done[t].sem, 1)
                for s in range(6):
                    for t in range(NT):
                        use = lv[s][t][1]
                        dve.wait_ge(use.filled, use.n + 1)
                        nc.vector.copy_predicated(
                            xt[:, t], bc3(levels[:, s + 1, :].bitcast(I32), 4),
                            use.ps[:, :].rearrange("p (h n) -> p h n", h=4)).then_inc(use.freed, 1)
                dve.wait_ge(uKS.filled, uKS.n + 1)
                dve.wait_ge(uV[1].freed, uV[1].n + 1)
                for hd in range(4):
                    ins = nc.vector.scalar_tensor_tensor(vb[1][:, hd, :], blk(uKS, hd),
                                                         nbek[:, 1, H0 + hd:H0 + hd + 1], vb[1][:, hd, :],
                                                         ALU.mult, ALU.add)
                ins.then_inc(uKS.freed, 1)
                split_lo(dve, z1.U)
                dve.wait_ge(uQS.freed, uQS.n + 1)
                dve.wait_ge(uO1.filled, uO1.n + 1)
                nc.vector.tensor_tensor(flat(dgb[:, 1]), uO1.ps[:, :], flat(yb[:, 0]), ALU.add)\
                    .then_inc(uO1.freed, 1)
                dve.wait_ge(o_ss.sem, o_ss.value)
                nc.vector.tensor_scalar(fo[:, :, H0:H0 + 4], sso[:, :, H0:H0 + 4], 1.0 / 128, EPS,
                                                    ALU.mult, ALU.add).then_inc(o_ms.sem, 1)
                dve.wait_ge(o_rt.sem, o_rt.value)
                nc.vector.tensor_tensor(fo[:, :, H0:H0 + 4], fo[:, :, H0:H0 + 4],
                                                      rq[:, :, H0:H0 + 4], ALU.mult)\
                                                          .then_inc(dve_self.sem, dve_self.add(1))
                dve.wait_ge(dve_self.sem, dve_self.n)
                for pr in range(2):
                    for e in range(2):
                        for t in range(NT):
                            hd = 2 * pr + e
                            ins = nc.vector.tensor_scalar(dgb[:, t, hd, :], dgb[:, t, hd, :],
                                                          fo[:, t, H0 + hd:H0 + hd + 1], None, ALU.mult)
                    ins.then_inc(on_d[pr].sem, 1)
                dve.wait_ge(z_silu.sem, z_silu.value)
                dve.wait_ge(z1.use.freed, z1.use.n + 1)
                for pr in range(2):
                    dve.wait_ge(uY[pr].filled, uY[pr].n + 1)
                    hs = slice(H0 + 2 * pr, H0 + 2 * pr + 2)
                    nc.vector.scalar_tensor_tensor(ytmp(pr), two(uY[pr].ps[:, :]), dn_gn, zt[:, hs, :],
                                                   ALU.mult, ALU.mult).then_inc(uY[pr].freed, 1)
                    dve.wait_ge(y_hi[pr].sem, y_hi[pr].value)
                    nc.vector.tensor_tensor(y_parts[pr][1], ytmp(pr), f32(y_parts[pr][0]), ALU.subtract)\
                        .then_inc(y_lo[pr].sem, 1)

            def pool_f(pool):
                for t in range(NT):
                    if before:
                        pool.wait_ge(before.on_d[1].sem, before.on_d[1].value)
                    nc.gpsimd.tensor_copy(xt[:, t], bc3(ident[:, :], 4)).then_inc(b_free[t].sem, 1)
                pool.wait_ge(o_ms.sem, o_ms.value)
                nc.gpsimd.tensor_tensor(fo[:, :, H0:H0 + 4], fo[:, :, H0:H0 + 4],
                                                    mhalf[:, 0:8].rearrange("p (t n) -> p t n", t=2), ALU.pow)\
                                                        .then_inc(o_rt.sem, 1)

            return Part(pe=pe_f, act=act_f, dve=dve_f, pool=pool_f, on_d=on_d, y=y_lo, last=z2, parts=y_parts)

        def rows_gemm(W, operands, ready, inner=None):
            n_units = len(operands)
            us = [unit(rows(W, 256 * k)) for k in range(n_units)]
            acc = [b.use() for b in O]

            def pe_f(pe):
                for k in range(n_units):
                    if inner and k == 2:
                        inner.pe(pe)
                    for sem_, value in ready[k]:
                        pe.wait_ge(sem_, value)
                    gemm_rows(pe, us[k], acc, *operands[k],
                              first=(k == 0), last=(k == n_units - 1))

            def act_f(act):
                for k, u in enumerate(us):
                    split_hi(act, u)
                    if inner and k == 0:
                        act_tiles(act, inner)
                    elif inner and k == 1:
                        inner.act_parts(act)

            def dve_f(dve):
                for k, u in enumerate(us):
                    split_lo(dve, u)
                    if inner and k == 0:
                        dve_tiles(dve, inner)
                    elif inner and k == 1:
                        inner.dve_parts(dve)

            return Part(pe=pe_f, act=act_f, dve=dve_f, acc=acc)

        def two(ap):
            return ap.rearrange("p (f t) -> p f t", f=2)

        def block_of(W, c0, bank, dst=None, tokens=False, scale=1.0, row=0):
            return Block(U=unit(features(W, c0, row)), use=bank.use(), dst=dst, tokens=tokens, scale=scale)

        def block_product(pe, b, ahi=xhi, alo=xlo):
            (gemm_tokens if b.tokens else gemm_features)(pe, b.U, b.use, ahi, alo)

        def block_copy(act, b):
            act.wait_ge(b.use.filled, b.use.n + 1)
            nc.scalar.activation(b.dst, b.use.ps[:, :], ACT.Copy, scale=b.scale).then_inc(b.use.freed, 1)

        def rows_of(ap, r):
            return ap if r is None else ap[r:r + 64]

        mx = sb("mx", [P, 48])
        head_rows = sb("head_rows", [P, 512])
        att_max = Signal(sem("att_max"))
        att_exp = Signal(sem("att_exp"))
        att_prob = Signal(sem("att_prob"))
        att_y = Signal(sem("att_y"))
        att_ss = Signal(sem("att_ss"))
        att_root = Signal(sem("att_root"))

        def attend(e, q_use, k_use, v_use, q, k, v, n_lane, kind, slopes=None, ydst=None,
                   extra_scores=None, full=False, vbanks=None, lbuf=None, scale=1.0):
            W_ = 512 if full else 384
            segs = [(0, 256), (256, 512)] if full else [(0, 128), (128, 384)]
            blocks = ([(0, 0, 0, 0), (1, 0, 256, 128), (0, 1, 128, 256), (1, 1, 384, 384)] if full
                      else [(0, 0, 0, 0), (1, 0, 128, 128), (1, 1, 256, 256)])
            us = [O[x].use() for x in range(n_lane)]
            t_lanes = [0, 2] if kind == "diff" else list(range(n_lane))
            ut = {x: O[x].use() for x in t_lanes}
            uv = [b.use() for b in vbanks]
            m_neg, e_done, p_done = att_max.next(), None if full else att_exp.next(), att_prob.next()
            y_hi = att_y.many(len(uv))
            buf = [lbuf[x] for x in range(n_lane)]
            mcol, scol = mx[:, 0:8], mx[:, 8:16]

            def pe_scores(pe):
                pe.wait_ge(q_use.freed, q_use.n + 1)
                pe.wait_ge(k_use.freed, k_use.n + 1)
                for x in range(n_lane):
                    if us[x].n:
                        pe.wait_ge(us[x].freed, us[x].n)
                    for t, (a_, b_) in enumerate(segs):
                        last = extra_scores is None
                        ins = pe.matmul(us[x].ps[:, a_:b_], q(x, t), k(x, 256 if full or t else 128),
                                        start=True, stop=last, skip_group_check=True)
                        if extra_scores:
                            ins = extra_scores(pe, us[x].ps[:, a_:b_], x, t)
                    ins.then_inc(us[x].filled, 1)

            def dve_max(dve):
                for x in range(n_lane):
                    dve.wait_ge(us[x].filled, us[x].n + 1)
                    if full:
                        nc.vector.tensor_reduce(
                            mcol[:, 2 * x:2 * x + 2], us[x].ps[:, :].rearrange("p (t n) -> p t n", t=2), AX,
                            ALU.max).then_inc(dve_self.sem, dve_self.add(1))
                        continue
                    slope = slopes(x) if slopes else 1.0
                    mask = amask if kind == "diff" else fmask
                    nc.vector.scalar_tensor_tensor(buf[x], mask, slope, us[x].ps[:, 0:W_],
                                                              ALU.mult, ALU.add).then_inc(us[x].freed, 1)
                for x in range(n_lane):
                    if full:
                        continue
                    dve.wait_ge(us[x].freed, us[x].n + 1)
                    for t, (a_, b_) in enumerate(segs):
                        nc.vector.tensor_reduce(mcol[:, 2 * x + t:2 * x + t + 1],
                                                              buf[x][:, a_:b_], AX, ALU.max)\
                                                                .then_inc(dve_self.sem, dve_self.add(1))
                dve.wait_ge(dve_self.sem, dve_self.n)
                nc.vector.tensor_scalar(mcol[:, 0:2 * n_lane], mcol[:, 0:2 * n_lane], -scale,
                                                     None, ALU.mult).then_inc(m_neg.sem, 1)

            def act_exp(act):
                act.wait_ge(m_neg.sem, m_neg.value)
                for x in range(n_lane):
                    for t, (a_, b_) in enumerate(segs):
                        src = us[x].ps[:, a_:b_] if full else buf[x][:, a_:b_]
                        c = 2 * x + t
                        ins = nc.scalar.activation(buf[x][:, a_:b_], src, ACT.Exp, bias=mcol[:, c:c + 1],
                                                   scale=scale, accum_out=scol[:, c:c + 1])
                        if full and t == 1:
                            ins.then_inc(us[x].freed, 1)
                if not full:
                    ins.then_inc(e_done.sem, 1)

            def dve_scale(dve):
                if full:
                    dve.wait_ge(us[n_lane - 1].freed, us[n_lane - 1].n + 1)
                else:
                    dve.wait_ge(e_done.sem, e_done.value)
                rc = mx[:, 24:24 + 2 * n_lane]
                nc.vector.reciprocal(rc, scol[:, 0:2 * n_lane]).then_inc(dve_self.sem, dve_self.add(1))
                dve.wait_ge(dve_self.sem, dve_self.n)
                if kind == "diff":
                    r2 = rc.rearrange("p (h c t) -> p h c t", h=2, c=2)
                    nc.vector.tensor_scalar(mx[:, 32:36].rearrange("p (h t) -> p h t", h=2),
                                                          r2[:, :, 1, :], lam, None, ALU.mult)\
                                                              .then_inc(dve_self.sem, dve_self.add(1))
                    dve.wait_ge(dve_self.sem, dve_self.n)
                    for hd in range(2):
                        for t, (a_, b_) in enumerate(segs):
                            c = 2 * hd + t
                            nc.vector.tensor_scalar(buf[2 * hd + 1][:, a_:b_],
                                                                  buf[2 * hd + 1][:, a_:b_],
                                                                  mx[:, 32 + c:33 + c], None, ALU.mult)\
                                                                .then_inc(dve_self.sem, dve_self.add(1))
                    dve.wait_ge(dve_self.sem, dve_self.n)
                    for hd in range(2):
                        for t, (a_, b_) in enumerate(segs):
                            c = 24 + 4 * hd + t
                            ins = nc.vector.scalar_tensor_tensor(buf[2 * hd][:, a_:b_], buf[2 * hd][:, a_:b_],
                                                                 mx[:, c:c + 1], buf[2 * hd + 1][:, a_:b_],
                                                                 ALU.mult, ALU.subtract)
                else:
                    for x in range(n_lane):
                        for t, (a_, b_) in enumerate(segs):
                            c = 24 + 2 * x + t
                            ins = nc.vector.tensor_scalar(buf[x][:, a_:b_], buf[x][:, a_:b_],
                                                          mx[:, c:c + 1], None, ALU.mult)
                ins.then_inc(p_done.sem, 1)

            def pe_turn(pe):
                pe.wait_ge(p_done.sem, p_done.value)
                for x in t_lanes:
                    if ut[x].n:
                        pe.wait_ge(ut[x].freed, ut[x].n)
                    for _, _, a_, b_ in blocks:
                        ins = pe.transpose(ut[x].ps[:, b_:b_ + P], buf[x][:, a_:a_ + P], ident[:, :])
                    ins.then_inc(ut[x].filled, 1)

            def act_turn(act):
                for x in t_lanes:
                    act.wait_ge(ut[x].filled, ut[x].n + 1)
                    nc.scalar.activation(buf[x], ut[x].ps[:, 0:W_], ACT.Copy).then_inc(ut[x].freed, 1)

            def pe_values(pe):
                if v_use:
                    pe.wait_ge(v_use.freed, v_use.n + 1)
                for n, x in enumerate(t_lanes):
                    pe.wait_ge(ut[x].freed, ut[x].n + 1)
                    if kind == "diff":
                        u = uv[n]
                        if u.n:
                            pe.wait_ge(u.freed, u.n)
                        pe.matmul(u.ps[:, 0:P], buf[x][:, 0:P], v(n, 0), start=True, stop=True,
                                  skip_group_check=True)
                        pe.matmul(u.ps[:, P:2 * P], buf[x][:, P:2 * P], v(n, 0), start=True, stop=False,
                                  skip_group_check=True)
                        pe.matmul(u.ps[:, P:2 * P], buf[x][:, 2 * P:3 * P], v(n, 1), start=False,
                                         stop=True, skip_group_check=True).then_inc(u.filled, 1)
                        continue
                    if kind == "half":
                        u, pr = uv[x // 2], slice(64 * (x % 2), 64 * (x % 2) + 64)
                        if x % 2 == 0:
                            if u.n:
                                pe.wait_ge(u.freed, u.n)
                        o = u.ps[pr]
                    elif full:
                        u = uv[x // 2]
                        if x % 2 == 0:
                            if u.n:
                                pe.wait_ge(u.freed, u.n)
                        o = u.ps[:, 256 * (x % 2):256 * (x % 2) + 256]
                    else:
                        u = uv[x]
                        if u.n:
                            pe.wait_ge(u.freed, u.n)
                        o = u.ps[:, :]
                    pe.matmul(o[:, 0:256], v(x, 0), buf[x][:, 0:256], start=True, stop=False,
                              skip_group_check=True)
                    if full:
                        ins = pe.matmul(o[:, 0:256], v(x, 1), buf[x][:, 256:512], start=False, stop=True,
                                        skip_group_check=True)
                    else:
                        ins = pe.matmul(o[:, P:2 * P], v(x, 1), buf[x][:, 256:384], start=False, stop=True,
                                        skip_group_check=True)
                    if not (kind == "half" or full) or x % 2 == 1:
                        ins.then_inc(u.filled, 1)

            w = 512 if full else 256

            if kind != "diff":
                def act_y(act):
                    for n, u in enumerate(uv):
                        act.wait_ge(u.filled, u.n + 1)
                        nc.scalar.activation(ydst(0, n), u.ps[:, 0:w], ACT.Copy).then_inc(y_hi[n].sem, 1)

                def dve_y(dve):
                    for n, u in enumerate(uv):
                        dve.wait_ge(y_hi[n].sem, y_hi[n].value)
                        nc.vector.tensor_tensor(ydst(1, n), u.ps[:, 0:w], f32(ydst(0, n)), ALU.subtract)\
                            .then_inc(u.freed, 1)

                return Attention(e=e, scores=pe_scores, max=dve_max, exp=act_exp, normalise=dve_scale, turn=pe_turn,
                            turned=act_turn, values=pe_values, y_hi=act_y, y_lo=dve_y,
                            diff=False, ready=[u.done for u in uv])

            o_ss, o_rt = att_ss.next(), att_root.next()
            msa, ra = mx[:, 36:40], mx[:, 40:44]
            uy = vbanks[0].use()

            def act_ss(act):
                for n in range(2):
                    act.wait_ge(uv[n].filled, uv[n].n + 1)
                    for t in range(NT):
                        c = 2 * n + t
                        ins = nc.scalar.activation(head_rows[:, n * T + t * P:n * T + (t + 1) * P],
                                                   uv[n].ps[:, t * P:(t + 1) * P], ACT.Square,
                                                   accum_out=msa[:, c:c + 1])
                ins.then_inc(o_ss.sem, 1)

            def pool_rt(pool):
                pool.wait_ge(o_ss.sem, o_ss.value)
                nc.gpsimd.tensor_scalar(msa, msa, 1.0 / P, EPS, ALU.mult, ALU.add)\
                    .then_inc(pool_self.sem, pool_self.add(1))
                pool.wait_ge(pool_self.sem, pool_self.n)
                nc.gpsimd.tensor_tensor(ra, msa, mhalf[:, 0:4], ALU.pow).then_inc(o_rt.sem, 1)

            def dve_on(dve):
                dve.wait_ge(o_rt.sem, o_rt.value)
                for n in range(2):
                    for t in range(NT):
                        ins = nc.vector.tensor_scalar(head_rows[:, n * T + t * P:n * T + (t + 1) * P],
                                                      uv[n].ps[:, t * P:(t + 1) * P],
                                                      ra[:, 2 * n + t:2 * n + t + 1], None, ALU.mult)
                    ins.then_inc(uv[n].freed, 1)

            def pe_on(pe):
                pe.wait_ge(uv[1].freed, uv[1].n + 1)
                if uy.n:
                    pe.wait_ge(uy.freed, uy.n)
                for n in range(2):
                    for t in range(NT):
                        ins = pe.transpose(uy.ps[:, n * T + t * P:n * T + (t + 1) * P],
                                           head_rows[:, n * T + t * P:n * T + (t + 1) * P],
                                               ident[:, :])
                ins.then_inc(uy.filled, 1)

            def act_y2(act):
                act.wait_ge(uy.filled, uy.n + 1)
                nc.scalar.activation(ydst(0, 0), uy.ps[:, :], ACT.Copy, scale=diff_g8).then_inc(y_hi[0].sem, 1)
                nc.scalar.activation(mx[:, 44:45], ra[:, 0:1], ACT.Copy).then_inc(y_hi[1].sem, 1)

            def dve_y2(dve):
                dve.wait_ge(y_hi[1].sem, y_hi[1].value)
                nc.vector.scalar_tensor_tensor(ydst(1, 0), uy.ps[:, :], diff_g8, f32(ydst(0, 0)),
                                                       ALU.mult, ALU.subtract).then_inc(uy.freed, 1)

            return Attention(e=e, scores=pe_scores, max=dve_max, exp=act_exp, normalise=dve_scale, turn=pe_turn,
                        turned=act_turn, values=pe_values, squares=act_ss, root=pool_rt, scaled=dve_on,
                        turn_y=pe_on, y_hi=act_y2, y_lo=dve_y2, diff=True, ready=[uy.done])

        def attention_pe(pe, a, e):
            if e == a.e:
                a.scores(pe)
            elif e == a.e + 2:
                a.turn(pe)
            elif e == a.e + 3:
                a.values(pe)
            elif e == a.e + 4 and a.diff:
                a.turn_y(pe)

        def attention_act_early(act, a, e):
            if e == a.e + 3:
                a.turned(act)
            elif e == a.e + 4:
                (a.squares if a.diff else a.y_hi)(act)
            elif e == a.e + 5 and a.diff:
                a.y_hi(act)

        def attention_act_late(act, a, e):
            if e == a.e + 1:
                a.exp(act)

        def attention_dve(dve, a, e):
            if e == a.e + 1:
                a.max(dve)
            elif e == a.e + 2:
                a.normalise(dve)
            elif e == a.e + 4:
                (a.scaled if a.diff else a.y_lo)(dve)
            elif e == a.e + 5 and a.diff:
                a.y_lo(dve)

        LAMBDA_INIT = 0.2
        lam = sml_rows[:, 280:281]
        diff_g8 = sml_rows[:, 281:282]

        def trio_views(n):
            b = trio[n % 2]
            return b[:, 0:512], b[:, 512:1024], b[:, 1024:1536]

        def tq(n, x, t, r=None):
            return rows_of(two(trio_views(n)[0])[:, x, t * P:(t + 1) * P], r)

        def moba(norm):
            W = A["mb_w_in"][0]
            blocks, heads = [], []
            for n in range(4):
                for j in range(3):
                    blocks.append(block_of(W, D * j + 256 * n, G[(3 * n + j) % 2], trio_views(n)[j], j == 2,
                                           128.0 ** -0.5 if j == 0 else 1.0))
            for n in range(4):
                qu, ku, vu = (b.use for b in blocks[3 * n:3 * n + 3])
                heads.append(attend(
                    3 * n + 2, qu, ku, vu,
                    q=lambda x, t, n=n: tq(n, x, t),
                    k=lambda x, w, n=n: two(trio_views(n)[1])[:, x, 0:w],
                    v=lambda x, t, n=n: trio_views(n)[2][:, t * T + x * P:t * T + (x + 1) * P],
                    n_lane=2, kind="whole", slopes=lambda x, n=n: 2.0 ** -(2 * n + x + 1),
                    ydst=lambda part, x, n=n: (bhi, blo)[part][:, 2 * n + x, :], vbanks=[G[2], G[3]],
                    lbuf=lanes))
            STEPS = len(blocks) + 3

            def pe_f(pe):
                wait_parts(pe, norm)
                for e in range(STEPS):
                    if e < len(blocks):
                        block_product(pe, blocks[e])
                    for a in heads:
                        attention_pe(pe, a, e)

            def act_f(act):
                for e in range(STEPS + 1):
                    for a in heads:
                        attention_act_early(act, a, e)
                    if e < len(blocks):
                        split_hi(act, blocks[e].U)
                    for a in heads:
                        attention_act_late(act, a, e)
                    if e < len(blocks):
                        block_copy(act, blocks[e])

            def dve_f(dve):
                for e in range(STEPS + 1):
                    for a in heads:
                        attention_dve(dve, a, e)
                    if e < len(blocks):
                        split_lo(dve, blocks[e].U)

            return Part(pe=pe_f, act=act_f, dve=dve_f, ready=[a.ready for a in heads])

        c_col = sm[:, 0:16]
        lf = sm[:, 16:32]
        lt = [sm[:, 32 + 16 * j:48 + 16 * j] for j in range(4)]

        def forget_gates(norm):
            ug, uc = O[0].use(), O[1].use()
            l_d, d_, u_d = d2a.many(3)
            l_a, a1, l1 = a2d.many(3)
            f_d = d2t.next()

            def pe_f(pe):
                wait_parts(pe, norm)
                pe.wait_ge(sm_lo2.sem, sm_lo2.value)
                if ug.n:
                    pe.wait_ge(ug.freed, ug.n)
                for t in range(NT):
                    for k in range(KT):
                        ts = slice(t * P, (t + 1) * P)
                        ins = mm3(pe, ug.ps[:, 8 * t:8 * t + 8], xhi[:, k, ts], xlo[:, k, ts],
                                  smh[:, k, 0:8], sml[:, k, 0:8], t == 0 and k == 0, t == 1 and k == KT - 1)
                ins.then_inc(ug.filled, 1)

            def pe_cum(pe):
                pe.wait_ge(f_d.sem, f_d.value)
                if uc.n:
                    pe.wait_ge(uc.freed, uc.n)
                pe.matmul(uc.ps[:, 0:8], upper[:, :], lf[:, 0:8], start=True, stop=True, skip_group_check=True)
                pe.matmul(uc.ps[:, 8:16], ones[:, :], lf[:, 0:8], start=True, stop=False, skip_group_check=True)
                pe.matmul(uc.ps[:, 8:16], upper[:, :], lf[:, 8:16], start=False, stop=True,
                                  skip_group_check=True).then_inc(uc.filled, 1)

            def act_f(act):
                act.wait_ge(l_d.sem, l_d.value)
                nc.scalar.activation(lam_in[:, 128:130], lam_in[:, 128:130], ACT.Exp).then_inc(l_a.sem, 1)
                act.wait_ge(d_.sem, d_.value)
                nc.scalar.activation(lt[1], lt[1], ACT.Exp, scale=-1.0).then_inc(a1.sem, 1)
                act.wait_ge(u_d.sem, u_d.value)
                nc.scalar.activation(lt[3], lt[2], ACT.Ln).then_inc(l1.sem, 1)

            def dve_f(dve):
                def link(ins):
                    ins.then_inc(dve_self.sem, dve_self.add(1))
                    dve.wait_ge(dve_self.sem, dve_self.n)

                pair = lam_in.rearrange("p (a b n) -> p a b n", a=2, b=2)
                link(nc.vector.tensor_tensor(pair[:, :, 0, :], pair[:, :, 0, :], pair[:, :, 1, :], ALU.mult))
                link(nc.vector.tensor_reduce(sml_rows[:, 282:284], pair[:, :, 0, :], AX, ALU.add))
                nc.vector.tensor_copy(lam_in[:, 128:130], sml_rows[:, 282:284]).then_inc(l_d.sem, 1)
                link(nc.vector.tensor_scalar(diff_g8, diff_g, 1.0 - LAMBDA_INIT, None, ALU.mult))
                dve.wait_ge(l_a.sem, l_a.value)
                link(nc.vector.tensor_tensor(lam, lam_in[:, 128:129], lam_in[:, 129:130], ALU.subtract))
                link(nc.vector.tensor_scalar(lam, lam, LAMBDA_INIT, None, ALU.add))
                dve.wait_ge(ug.filled, ug.n + 1)
                t2 = lambda a: a.rearrange("p (t n) -> p t n", t=2)
                nc.vector.tensor_tensor(t2(lt[0]), t2(ug.ps[:, 0:16]), bc3(bfgt, 2), ALU.add)\
                    .then_inc(ug.freed, 1)
                dve.wait_ge(ug.freed, ug.n + 1)
                link(nc.vector.tensor_scalar(lt[1], lt[0], -1.0, None, ALU.mult))
                nc.vector.tensor_tensor(lt[1], lt[1], lt[0], ALU.max).then_inc(d_.sem, 1)
                link(nc.vector.tensor_scalar(lt[0], lt[0], 0.0, None, ALU.min))
                dve.wait_ge(a1.sem, a1.value)
                nc.vector.tensor_scalar(lt[2], lt[1], 1.0, None, ALU.add).then_inc(u_d.sem, 1)
                dve.wait_ge(u_d.sem, u_d.value)
                link(nc.vector.tensor_scalar(lf, lt[2], -1.0, None, ALU.add))
                link(nc.vector.tensor_tensor(lt[1], lt[1], lf, ALU.subtract))
                link(nc.vector.tensor_tensor(lt[0], lt[0], lt[1], ALU.subtract))
                dve.wait_ge(l1.sem, l1.value)
                nc.vector.tensor_tensor(lf, lt[0], lt[3], ALU.subtract).then_inc(f_d.sem, 1)

            def dve_cum(dve):
                dve.wait_ge(uc.filled, uc.n + 1)
                nc.vector.tensor_copy(c_col, uc.ps[:, 0:16]).then_inc(uc.freed, 1)

            return Part(pe=pe_f, act=act_f, dve=dve_f, pe_cum=pe_cum, dve_cum=dve_cum, uc=uc)

        def block2(norm, gates0):
            W = A["w_in_2"][0]
            WG, WB = A["w_gate_2"][0], A["w_branch_2"][0].rearrange("n k d -> (n k) d")
            WO = A["w_out_2"][0]
            C0 = 3080
            turn = [0]

            def bank():
                turn[0] += 1
                return G[(turn[0] - 1) % 2]

            SHORT, CONV, TRIO, MIX = 0, 6, 10, 22
            S = []

            sx, sbb = common[:, 0:1024], common[:, 1024:2048]
            su = common[:, 3072:3072 + 4 * 258].rearrange("p (f t) -> p f t", f=4)
            sy = conv_y
            pads = p2d.next()
            for j in range(4):
                dst = (sx if j < 2 else sbb)[:, 512 * (j % 2):512 * (j % 2) + 512]
                S.append(block_of(W, C0 + 1024 + 256 * j, bank(), dst))
            for j in range(2):
                S.append(block_of(W, C0 + 2048 + 256 * j, bank()))
            ys_d, ys_h, ys_lo = (Signal(sem(n_)).next() for n_ in ("short_f32", "short_hi", "short_lo"))

            def dve_short_product(dve, j):
                b, x = S[SHORT + 4 + j], S[SHORT + j]
                dve.wait_ge(b.use.filled, b.use.n + 1)
                dve.wait_ge(x.use.freed, x.use.n + 1)
                dve.wait_ge(pads.sem, pads.value)
                nc.vector.tensor_tensor(su[:, 2 * j:2 * j + 2, 2:], two(b.use.ps[:, :]),
                                        two(sx[:, 512 * j:512 * j + 512]), ALU.mult).then_inc(b.use.freed, 1)

            def dve_short_conv(dve):
                for b in S[SHORT + 4:SHORT + 6]:
                    dve.wait_ge(b.use.freed, b.use.n + 1)
                for tap in (2, 1, 0):
                    if tap < 2:
                        dve.wait_ge(dve_self.sem, dve_self.n)
                    for f in range(4):
                        sh = su[:, f, tap:tap + T]
                        wc = sc_w[:, tap, f:f + 1]
                        if tap == 2:
                            ins = nc.vector.tensor_scalar(sy[:, f, :], sh, wc, None, ALU.mult)
                        else:
                            ins = nc.vector.scalar_tensor_tensor(sy[:, f, :], sh, wc, sy[:, f, :],
                                                                 ALU.mult, ALU.add)
                        ins.then_inc(dve_self.sem, dve_self.add(1))
                dve.wait_ge(dve_self.sem, dve_self.n)
                for b in S[SHORT + 2:SHORT + 4]:
                    dve.wait_ge(b.use.freed, b.use.n + 1)
                nc.vector.tensor_tensor(sbb, sbb, sy.rearrange("p f t -> p (f t)"), ALU.mult)\
                    .then_inc(ys_d.sem, 1)

            def act_short_hi(act):
                act.wait_ge(ys_d.sem, ys_d.value)
                nc.scalar.activation(bhi[:, 12:16, :].rearrange("p f t -> p (f t)"), sbb, ACT.Copy)\
                    .then_inc(ys_h.sem, 1)

            def dve_short_lo(dve):
                dve.wait_ge(ys_h.sem, ys_h.value)
                nc.vector.tensor_tensor(blo[:, 12:16, :].rearrange("p f t -> p (f t)"), sbb,
                                        f32(bhi[:, 12:16, :].rearrange("p f t -> p (f t)")),
                                        ALU.subtract).then_inc(ys_lo.sem, 1)

            sgc = common[:, 2048:3072]
            for j in range(4):
                S.append(block_of(W, C0 + 256 * j, bank()))

            def act_glu(act, j):
                b = S[CONV + j]
                act.wait_ge(b.use.filled, b.use.n + 1)
                if j == 0:
                    act.wait_ge(pads.sem, pads.value)
                for f in range(2):
                    c = 2 * j + f
                    dst = conv_u[:, c, 30:] if j < 2 else sgc[:, 256 * (c - 4):256 * (c - 4) + 256]
                    ins = nc.scalar.activation(dst, b.use.ps[:, f * T:(f + 1) * T],
                                               ACT.Identity if j < 2 else ACT.Sigmoid,
                                               bias=b_glu[:, c:c + 1])
                ins.then_inc(b.use.freed, 1)

            def dve_glu(dve, j):
                b, fs = S[CONV + 2 + j], slice(2 * j, 2 * j + 2)
                dve.wait_ge(b.use.freed, b.use.n + 1)
                nc.vector.tensor_tensor(conv_u[:, fs, 30:], conv_u[:, fs, 30:],
                                        two(sgc[:, 512 * j:512 * j + 512]), ALU.mult)\
                    .then_inc(u_ready[j].sem, 1)

            for n in range(4):
                base = 0 if n < 2 else 1536
                for j in range(3):
                    S.append(block_of(W, base + 512 * j + 256 * (n % 2), bank(), trio_views(n)[j], j == 2,
                                      0.125 if j == 0 else 1.0))
            assert len(S) == MIX
            scores_at = [TRIO + 2 + 3 * n for n in range(4)]

            DVE_TILES = 3
            taps = [(j, f) for j in range(31) for f in range(DVE_TILES)]
            quota = [16, 16, 3] + 3 * [7, 12, 3]
            quota = [sum(quota[:n]) for n in range(len(quota) + 1)]
            assert len(quota) == MIX - TRIO + 1 and quota[-1] >= len(taps)
            y_conv = Signal(sem("conv_summed")).next()
            y_conv_pool = Signal(sem("conv_summed_pool")).next()
            u_ready = Signal(sem("conv_u_ready")).many(2)

            def dve_taps(dve, n):
                if n == 0:
                    dve.wait_ge(u_ready[1].sem, u_ready[1].value)
                for j, f in taps[quota[n]:quota[n + 1]]:
                    if f == 0 and j:
                        dve.wait_ge(dve_self.sem, dve_self.n)
                    src = conv_u[:, f, j:j + T]
                    if j == 0:
                        ins = nc.vector.tensor_scalar(conv_y[:, f, :], src, dw_w[:, j, f:f + 1],
                                                      dw_b[:, f:f + 1], ALU.mult, ALU.add)
                    else:
                        ins = nc.vector.scalar_tensor_tensor(conv_y[:, f, :], src, dw_w[:, j, f:f + 1],
                                                             conv_y[:, f, :], ALU.mult, ALU.add)
                    if (j, f) == taps[-1]:
                        ins.then_inc(y_conv.sem, 1)
                    else:
                        ins.then_inc(dve_self.sem, dve_self.add(1))

            def pool_taps(pool, j0, j1):
                fs = slice(DVE_TILES, 4)
                shape = (P, 4 - DVE_TILES, T)
                y = conv_y[:, fs, :]
                for j in range(j0, j1):
                    product = pool_product[:, j % 2, 0:4 - DVE_TILES, :]
                    nc.gpsimd.tensor_tensor(product, conv_u[:, fs, j:j + T],
                                            dw_w[:, j, fs].unsqueeze(2).broadcast_to(shape), ALU.mult)\
                        .then_inc(pool_self.sem, pool_self.add(1))
                    pool.wait_ge(pool_self.sem, pool_self.n)
                    before = y if j else dw_b[:, fs].unsqueeze(2).broadcast_to(shape)
                    ins = nc.gpsimd.tensor_tensor(y, product, before, ALU.add)
                    if j == 30:
                        ins.then_inc(y_conv_pool.sem, 1)
                    else:
                        ins.then_inc(pool_self.sem, pool_self.add(1))

            diag_done = Signal(sem("diag_done")).many(2)

            def dve_diag(dve, m):
                dve.wait_ge(gates0.uc.freed, gates0.uc.n + 1)
                for x in range(4):
                    for t in range(NT):
                        c = 8 * t + 4 * m + x
                        ins = nc.vector.tensor_scalar(diag_f[:, 2 * x + t, :], ident[:, :], c_col[:, c:c + 1],
                                                      None, ALU.mult)
                ins.then_inc(diag_done[m].sem, 1)

            def gate_scores(pe, o, x, t, m):
                if x == 0 and t == 0:
                    pe.wait_ge(diag_done[m].sem, diag_done[m].value)
                rhs = diag_f[:, 2 * x:2 * x + 1 + t, :].rearrange("p b n -> p (b n)")
                return pe.matmul(o, nones[:, :], rhs, start=False, stop=True, skip_group_check=True)

            added = Signal(sem("branch_added"))
            prods, hi_m, lo_m = [], [], []
            sg = [common[:, 512 * g:512 * g + 512] for g in range(3)] + [common[:, 6776:6776 + 512]]
            macc = common[:, 6776 + 512:6776 + 1024]
            heads, acc, gate_uses, ln = [], [], [], []
            gate_at, branch_at, rows_at = {}, {}, {}
            for j in range(4):
                prods.append(added.many(3))
                for g in range(4):
                    if j == 0 and g % 2 == 1:
                        ln.append(bank().use())
                    gate_at[len(S)] = (j, g)
                    S.append(block_of(WG, D * g + 256 * j, bank()))
                    gate_uses.append(S[-1].use)
                    if g == 1 and j:
                        if j == 1:
                            acc.extend(b.use() for b in O)
                        rows_at[len(S)] = j - 1
                        S.append(Block(U=unit(rows(WO, 256 * (j - 1)))))
                if j == 0:
                    ln.append(bank().use())
                    for n in range(4):
                        diff, m = n < 2, n - 2
                        qu, ku, vu = (b.use for b in S[TRIO + 3 * n:TRIO + 3 * n + 3])
                        views = trio_views(n)
                        width = P if diff else 64
                        heads.append(attend(
                            scores_at[n], qu, ku, vu,
                            q=lambda x, t, n=n: tq(n, x // 2, t, 64 * (x % 2)),
                            k=lambda x, w, views=views: two(views[1])[64 * (x % 2):64 * (x % 2) + 64, x // 2, 0:w],
                            v=lambda x, t, views=views, width=width: views[2][:, t * T + width * x:
                                                                              t * T + width * (x + 1)],
                            n_lane=4, kind="diff" if diff else "half", vbanks=[G[2], G[3]], lbuf=lanes,
                            extra_scores=None if diff else (lambda pe, o, x, t, m=m: gate_scores(pe, o, x, t, m)),
                            ydst=(lambda part, _, n=n: (bhi, blo)[part][:, 2 * n:2 * n + 2, :].rearrange(
                                "p f t -> p (f t)")) if diff else
                            (lambda part, p_, m=m: (bhi, blo)[part][:, 4 + 2 * m + p_, :])))
                for b in range(2):
                    branch_at[len(S)] = (j, b)
                    S.append(Block(U=unit(features(WB, 256 * j, row=D * b)), uses=[G[2 + b].use(), bank().use()]))
                hi_m.append(hid_sq.next())
                lo_m.append(hid_lo.next())
            rows_at[len(S)] = 3
            S.append(Block(U=unit(rows(WO, 256 * 3))))

            um, uvv, ur = ln
            sq_a = a2t.next()
            r_p = Signal(sem("conv_root")).next()
            r_d, n_d, s_a, y_lo = (Signal(sem(n_)).next()
                                   for n_ in ("conv_root_diag", "conv_normed", "conv_hi", "conv_lo"))
            sqv = conv_u.rearrange("p f t -> p (f t)")[:, 0:1024].rearrange("p (f t) -> p f t", f=4)
            roots = sqv[:, 0, :]
            var, root = mx[:, 16:18], mx[:, 18:20]

            def pe_mean(pe):
                pe.wait_ge(y_conv.sem, y_conv.value)
                pe.wait_ge(y_conv_pool.sem, y_conv_pool.value)
                if um.n:
                    pe.wait_ge(um.freed, um.n)
                for f in range(4):
                    ins = pe.matmul(um.ps[:, 0:T], ones[:, :], conv_y[:, f, :], start=(f == 0), stop=(f == 3))
                ins.then_inc(um.filled, 1)

            def dve_centre(dve):
                dve.wait_ge(um.filled, um.n + 1)
                for f in range(4):
                    ins = nc.vector.scalar_tensor_tensor(conv_y[:, f, :], um.ps[:, 0:T], -1.0 / 512,
                                                         conv_y[:, f, :], ALU.mult, ALU.add)
                ins.then_inc(um.freed, 1)

            def act_square(act):
                act.wait_ge(um.freed, um.n + 1)
                nc.scalar.activation(sqv, conv_y, ACT.Square).then_inc(sq_a.sem, 1)

            def pe_var(pe):
                pe.wait_ge(sq_a.sem, sq_a.value)
                if uvv.n:
                    pe.wait_ge(uvv.freed, uvv.n)
                for t in range(NT):
                    for f in range(4):
                        ins = pe.matmul(uvv.ps[:, t:t + 1], sqv[:, f, t * P:(t + 1) * P], ones[:, 0:1],
                                        start=(t == 0 and f == 0), stop=(t == 1 and f == 3),
                                        skip_group_check=True)
                ins.then_inc(uvv.filled, 1)

            def dve_var(dve):
                dve.wait_ge(uvv.filled, uvv.n + 1)
                nc.vector.tensor_scalar(var, uvv.ps[:, 0:2], 1.0 / 512, EPS, ALU.mult, ALU.add)\
                    .then_inc(uvv.freed, 1)

            def pool_root(pool):
                pool.wait_ge(uvv.freed, uvv.n + 1)
                nc.gpsimd.tensor_tensor(root, var, mhalf[:, 0:2], ALU.pow).then_inc(r_p.sem, 1)

            def dve_root_diag(dve):
                dve.wait_ge(r_p.sem, r_p.value)
                for t in range(NT):
                    ins = nc.vector.tensor_scalar(roots[:, t * P:(t + 1) * P], ident[:, :], root[:, t:t + 1],
                                                  None, ALU.mult)
                ins.then_inc(r_d.sem, 1)

            def pe_spread(pe):
                pe.wait_ge(r_d.sem, r_d.value)
                if ur.n:
                    pe.wait_ge(ur.freed, ur.n)
                pe.matmul(ur.ps[:, 0:T], ones[:, :], roots, start=True, stop=True).then_inc(ur.filled, 1)

            def dve_norm(dve):
                dve.wait_ge(ur.filled, ur.n + 1)
                for f in range(4):
                    ins = nc.vector.tensor_tensor(conv_y[:, f, :], conv_y[:, f, :], ur.ps[:, 0:T], ALU.mult)
                ins.then_inc(ur.freed, 1)

            def act_silu(act):
                act.wait_ge(ur.freed, ur.n + 1)
                for f in range(4):
                    ins = nc.scalar.activation(conv_y[:, f, :], conv_y[:, f, :], ACT.Silu,
                                               scale=ln_g[:, f:f + 1], bias=ln_b[:, f:f + 1])
                ins.then_inc(act_self.sem, act_self.add(1))
                act.wait_ge(act_self.sem, act_self.n)
                nc.scalar.activation(bhi[:, 8:12, :], conv_y, ACT.Copy).then_inc(s_a.sem, 1)

            def dve_lo(dve):
                dve.wait_ge(s_a.sem, s_a.value)
                nc.vector.tensor_tensor(blo[:, 8:12, :], conv_y, f32(bhi[:, 8:12, :]), ALU.subtract)\
                    .then_inc(y_lo.sem, 1)

            branch_ready = [heads[0].ready + heads[1].ready, heads[2].ready + heads[3].ready,
                            [y_lo.done], [ys_lo.done]]

            def act_gate(act, e):
                j, g = gate_at[e]
                use = S[e].use
                act.wait_ge(use.filled, use.n + 1)
                if j:
                    m = prods[j - 1][max(g, 1) - 1]
                    act.wait_ge(m.sem, m.value)
                for f in range(2):
                    c = 8 * g + 2 * j + f
                    ins = nc.scalar.activation(sg[g][:, f * T:(f + 1) * T], use.ps[:, f * T:(f + 1) * T],
                                               ACT.Sigmoid, bias=b_gate[:, c:c + 1])
                ins.then_inc(use.freed, 1)

            def dve_branches(dve, e):
                j, b = branch_at[e]
                uses = S[e].uses
                for c in range(2):
                    n = 2 * b + c
                    gate = gate_uses[4 * j + n]
                    dve.wait_ge(uses[c].filled, uses[c].n + 1)
                    dve.wait_ge(gate.freed, gate.n + 1)
                    if n == 0:
                        nc.vector.tensor_tensor(macc, uses[c].ps[:, :], sg[0], ALU.mult)\
                            .then_inc(uses[c].freed, 1)
                        continue
                    nc.vector.tensor_tensor(sg[n], uses[c].ps[:, :], sg[n], ALU.mult).then_inc(uses[c].freed, 1)
                    dve.wait_ge(uses[c].freed, uses[c].n + 1)
                    if n == 1:
                        dve.wait_ge(uses[0].freed, uses[0].n + 1)
                    else:
                        dve.wait_ge(prods[j][n - 2].sem, prods[j][n - 2].value)
                    nc.vector.tensor_tensor(macc, macc, sg[n], ALU.add).then_inc(prods[j][n - 1].sem, 1)

            def pe_f(pe):
                wait_parts(pe, norm)
                for e, b in enumerate(S):
                    if e in rows_at:
                        j = rows_at[e]
                        pe.wait_ge(lo_m[j].sem, lo_m[j].value)
                        gemm_rows(pe, b.U, acc, hhi[:, j % 2], hlo[:, j % 2], first=(j == 0), last=(j == 3))
                    elif e in branch_at:
                        j, half = branch_at[e]
                        for c in range(2):
                            n = 2 * half + c
                            if j == 0:
                                for sem_, value in branch_ready[n]:
                                    pe.wait_ge(sem_, value)
                            gemm_features(pe, b.U, b.uses[c], bhi[:, 4 * n:4 * n + 4, :], blo[:, 4 * n:4 * n + 4, :],
                                          kts=4, wk0=4 * c, begins=(c == 0))
                    else:
                        block_product(pe, b)
                    if e == SHORT:
                        gates0.pe_cum(pe)
                    for a in heads:
                        attention_pe(pe, a, e)
                    if e == MIX:
                        pe_mean(pe)
                    elif e == MIX + 2:
                        pe_var(pe)
                    elif e == MIX + 3:
                        pe_spread(pe)

            def act_f(act):
                for e, b in enumerate(S):
                    for a in heads:
                        attention_act_early(act, a, e)
                    split_hi(act, b.U)
                    for a in heads:
                        attention_act_late(act, a, e)
                    if e == MIX + 4:
                        act_silu(act)
                    if TRIO <= e < TRIO + 3:
                        act.wait_ge(ys_lo.sem, ys_lo.value)
                    if CONV <= e < TRIO:
                        act_glu(act, e - CONV)
                    elif e in gate_at:
                        act_gate(act, e)
                    elif e < MIX and b.dst is not None:
                        block_copy(act, b)
                    if e == CONV:
                        act_short_hi(act)
                    if e == MIX + 2:
                        act_square(act)
                    if e in branch_at and branch_at[e][1]:
                        j = branch_at[e][0]
                        act.wait_ge(prods[j][2].sem, prods[j][2].value)
                        nc.scalar.activation(hhi[:, j % 2].rearrange("p k n -> p (k n)"), macc, ACT.Copy)\
                            .then_inc(hi_m[j].sem, 1)

            def dve_f(dve):
                for e, b in enumerate(S):
                    for a in heads:
                        attention_dve(dve, a, e)
                    split_lo(dve, b.U)
                    if e == CONV:
                        dve_short_conv(dve)
                    elif e == CONV + 1:
                        dve_short_lo(dve)
                    if e == MIX + 3:
                        dve_var(dve)
                    elif e == MIX + 4:
                        dve_norm(dve)
                    if SHORT + 4 <= e < CONV:
                        dve_short_product(dve, e - SHORT - 4)
                    elif CONV + 2 <= e < TRIO:
                        dve_glu(dve, e - CONV - 2)
                    elif e in branch_at:
                        if e == MIX + 4:
                            dve_lo(dve)
                        dve_branches(dve, e)
                    if e == SHORT + 1:
                        gates0.dve_cum(dve)
                    if TRIO <= e < MIX:
                        dve_taps(dve, e - TRIO)
                    for m in range(2):
                        if e == scores_at[2 + m] - 1:
                            dve_diag(dve, m)
                    if e == MIX + 1:
                        dve_centre(dve)
                    elif e == MIX + 3:
                        dve_root_diag(dve)
                    if e in branch_at and branch_at[e][1]:
                        j = branch_at[e][0]
                        dve.wait_ge(hi_m[j].sem, hi_m[j].value)
                        nc.vector.tensor_tensor(hlo[:, j % 2].rearrange("p k n -> p (k n)"), macc,
                                                f32(hhi[:, j % 2].rearrange("p k n -> p (k n)")),
                                                ALU.subtract).then_inc(lo_m[j].sem, 1)

            def pool_f(pool):
                for use in norm.parts:
                    pool.wait_ge(use.freed, use.n + 1)
                nc.gpsimd.memset(conv_u[:, :, 0:30], 0.0).then_inc(pool_self.sem, pool_self.add(1))
                pool.wait_ge(pool_self.sem, pool_self.n)
                nc.gpsimd.memset(su[:, :, 0:2], 0.0).then_inc(pads.sem, 1)
                pool.wait_ge(u_ready[1].sem, u_ready[1].value)
                pool_taps(pool, 0, 12)
                heads[0].root(pool)
                pool_taps(pool, 12, 20)
                heads[1].root(pool)
                pool_taps(pool, 20, 31)
                pool_root(pool)

            return Part(pe=pe_f, act=act_f, dve=dve_f, pool=pool_f, acc=acc)

        def memory_block(j, norm):
            xm = bhi[:, 8:16, :], blo[:, 8:16, :]
            b = block_of(A["w_xkv_2"][0], 256 * j, G[3 if j < 3 else 2], tokens=j >= 2)

            def pe_f(pe):
                wait_parts(pe, norm)
                block_product(pe, b, *xm)

            def act_f(act):
                split_hi(act, b.U)
                act.wait_ge(b.use.filled, b.use.n + 1)
                dst = xk[:, 2 * j:2 * j + 2, :] if j < 2 else xv[:, :, 256 * (j - 2):256 * (j - 1)]
                nc.scalar.activation(dst, two(b.use.ps[:, :]), ACT.Copy).then_inc(b.use.freed, 1)

            def dve_f(dve):
                split_lo(dve, b.U)

            return Part(pe=pe_f, act=act_f, dve=dve_f, last=b.use)

        def cross_attention(norm, kv):
            W = A["w_xq_2"][0]
            blocks = [block_of(W, 256 * j, G[j % 2], common[:, 512 * j:512 * j + 512]) for j in range(2)]
            qv = common[:, 0:1024].rearrange("p (f t) -> p f t", f=4)
            pb = [common[:, 3072 + 512 * x:3072 + 512 * x + 512] for x in range(4)]
            a = attend(1, blocks[1].use, blocks[0].use, kv.last,
                       q=lambda x, t: qv[:, x, t * P:(t + 1) * P], k=lambda x, w: xk[:, x, :],
                       v=lambda x, t: xv[:, t, x * P:(x + 1) * P], n_lane=4, kind="whole", full=True,
                       vbanks=[G[2], G[3]], lbuf=pb, scale=128.0 ** -0.5,
                       ydst=lambda part, p_: (bhi, blo)[part][:, 2 * p_:2 * p_ + 2, :].rearrange(
                           "p f t -> p (f t)"))

            def pe_f(pe):
                wait_parts(pe, norm)
                for b in blocks:
                    block_product(pe, b)
                a.scores(pe)
                a.turn(pe)
                a.values(pe)

            def act_f(act):
                for b in blocks:
                    split_hi(act, b.U)
                    block_copy(act, b)
                a.exp(act)
                a.turned(act)
                a.y_hi(act)

            def dve_f(dve):
                for b in blocks:
                    split_lo(dve, b.U)
                a.max(dve)
                a.normalise(dve)
                a.y_lo(dve)

            return Part(pe=pe_f, act=act_f, dve=dve_f, ready=[[r] for r in a.ready])

        def conv_mlp(norm):
            W, WD = A["w_up_2"][0], A["w_down_2"][0]
            FF = WD.shape[0]
            NB = FF // 256
            tail = (NB - 2) % 4
            loop = (NB - 2) // 4
            assert NB == 2 + 4 * loop + tail
            acc = []
            cg = [common[:, 512 * b_:512 * b_ + 512] for b_ in range(4)]
            prod = [common[:, 2048 + 512 * b_:2560 + 512 * b_] for b_ in range(2)]

            y1 = Signal(sem("ffn_first_tap"))
            sl = Signal(sem("ffn_silu"))
            mid = Signal(sem("ffn_mid"))
            pr = Signal(sem("ffn_prod"))

            def w_ap(tap, ft, per=0, i=0):
                if per:
                    return ffn_w[:, tap, bass.ds(ft + per * i, 1)]
                return ffn_w[:, tap, ft:ft + 1]

            def b_ap(ft, per=0, i=0):
                return ffn_b[:, bass.ds(ft + per * i, 1)] if per else ffn_b[:, ft:ft + 1]

            class Blk:

                def __init__(self, p_, ft, n, us, marks, uses):
                    self.p, self.ft, self.n, self.us = p_, ft, n, us
                    self.y1, self.mid, self.sl, self.pr, self.hi, self.lo = marks
                    self.uses = uses

            def act_half(act, b, half, i):
                split_hi(act, b.us[half], b.n, i)
                use, dst = b.uses[half], cg[2 * half + b.p]
                act.wait_ge(use.filled, use.at(i) + 1)
                per = 8 if b.n else 0
                for f in range(2):
                    ft = b.ft + f + half * (FF // P)
                    ins = nc.scalar.activation(dst[:, f * T:(f + 1) * T], use.ps[:, f * T:(f + 1) * T],
                                               ACT.Identity, scale=w_ap(2, ft, per, i), bias=b_ap(ft, per, i))
                ins.then_inc(b.y1[half].sem, 1)

            def act_block(act, b, i):
                act.wait_ge(b.uses[0].freed, b.uses[0].at(i) + 1)
                nc.scalar.activation(cg[b.p], cg[b.p], ACT.Silu).then_inc(b.sl.sem, 1)

            def act_hi(act, b, i):
                act.wait_ge(b.pr.sem, b.pr.at(i))
                nc.scalar.activation(hhi[:, b.p].rearrange("p k n -> p (k n)"), prod[b.p], ACT.Copy)\
                    .then_inc(b.hi.sem, 1)

            def dve_half(dve, b, half, i):
                split_lo(dve, b.us[half], b.n, i)
                use, dst = b.uses[half], cg[2 * half + b.p]
                dve.wait_ge(b.y1[half].sem, b.y1[half].at(i))
                per = 8 if b.n else 0
                for tap, sh in ((1, 1), (0, 2)):
                    if tap == 0:
                        dve.wait_ge(b.mid[half].sem, b.mid[half].at(i))
                    for f in range(2):
                        ft = b.ft + f + half * (FF // P)
                        ins = nc.vector.scalar_tensor_tensor(
                            dst[:, f * T + sh:(f + 1) * T], use.ps[:, f * T:(f + 1) * T - sh],
                            w_ap(tap, ft, per, i), dst[:, f * T + sh:(f + 1) * T], ALU.mult, ALU.add)
                    if tap == 1:
                        ins.then_inc(b.mid[half].sem, 1)
                ins.then_inc(use.freed, 1)

            def dve_block(dve, b, i):
                dve.wait_ge(b.sl.sem, b.sl.at(i))
                dve.wait_ge(b.uses[1].freed, b.uses[1].at(i) + 1)
                nc.vector.tensor_tensor(prod[b.p], cg[b.p], cg[2 + b.p], ALU.mult).then_inc(b.pr.sem, 1)
                dve.wait_ge(b.hi.sem, b.hi.at(i))
                nc.vector.tensor_tensor(hlo[:, b.p].rearrange("p k n -> p (k n)"), prod[b.p],
                                                    f32(hhi[:, b.p].rearrange("p k n -> p (k n)")),
                                                    ALU.subtract).then_inc(b.lo.sem, 1)

            def static_block(j):
                us = [unit(features(W, 256 * j)), unit(features(W, FF + 256 * j))]
                marks = (y1.many(2), mid.many(2), sl.next(), pr.next(), hid_sq.next(), hid_lo.next())
                uses = [G[2 * (j % 2) + k].use() for k in range(2)]
                b = Blk(j % 2, 2 * j, 0, us, marks, uses)
                return b

            b0, b1 = static_block(0), static_block(1)
            d0 = unit(rows(WD, 0))
            srcs = []
            for k in range(4):
                srcs += [lambda i, k=k: features(W, 512 + 256 * k + 1024 * i),
                         lambda i, k=k: features(W, FF + 512 + 256 * k + 1024 * i),
                         lambda i, k=k: rows(WD, 256 + 256 * k + 1024 * i)]
            L = unit_loop(loop, srcs)
            y1l, midl = y1.loop(loop, 8), mid.loop(loop, 8)
            sll, prl, hil, lol = (x.loop(loop, 4) for x in (sl, pr, hid_sq, hid_lo))
            gl = [G[b_].loop(loop, 2) for b_ in range(4)]
            lb = []
            for k in range(4):
                uses = [gl[2 * (k % 2)][k // 2], gl[2 * (k % 2) + 1][k // 2]]
                b = Blk(k % 2, 4 + 2 * k, 12, L[3 * k:3 * k + 2],
                        (y1l[2 * k:2 * k + 2], midl[2 * k:2 * k + 2], sll[k], prl[k], hil[k], lol[k]), uses)
                lb.append(b)
            tb, td = [], []
            for k in range(tail):
                tb.append(static_block(NB - tail + k))
                td.append(unit(rows(WD, 256 * (NB - tail + k - 1))))
            dl = unit(rows(WD, 256 * (NB - 1)))
            acc = [b.use() for b in O]

            def pe_block(pe, b, i=0):
                for half in range(2):
                    gemm_features(pe, b.us[half], b.uses[half], xhi, xlo, b.n, i)

            def pe_f(pe):
                wait_parts(pe, norm)
                pe_block(pe, b0)
                pe_block(pe, b1)
                pe.wait_ge(b0.lo.sem, b0.lo.value)
                gemm_rows(pe, d0, acc, hhi[:, 0], hlo[:, 0], first=True)
                with pe.Fori(0, loop) as i:
                    for k in range(4):
                        pe_block(pe, lb[k], i)
                        pe.wait_ge(hid_lo.sem, b1.lo.value + k + 4 * i)
                        q = (k + 1) % 2
                        gemm_rows(pe, L[3 * k + 2], acc, hhi[:, q], hlo[:, q], n=12, i=i)
                prev = hid_lo.sem, b1.lo.value + 4 * loop
                for k in range(tail):
                    pe_block(pe, tb[k])
                    pe.wait_ge(prev[0], prev[1] + k)
                    q = (k + 1) % 2
                    gemm_rows(pe, td[k], acc, hhi[:, q], hlo[:, q])
                pe.wait_ge(prev[0], prev[1] + tail)
                q = (NB - 1) % 2
                gemm_rows(pe, dl, acc, hhi[:, q], hlo[:, q], last=True)

            def act_all(act, b, dunit, n, i=0):
                act_half(act, b, 0, i)
                act_half(act, b, 1, i)
                act_block(act, b, i)
                if dunit is not None:
                    split_hi(act, dunit, n, i)
                act_hi(act, b, i)

            def dve_all(dve, b, dunit, n, i=0):
                dve_half(dve, b, 0, i)
                dve_half(dve, b, 1, i)
                if dunit is not None:
                    split_lo(dve, dunit, n, i)
                dve_block(dve, b, i)

            def act_f(act):
                act_all(act, b0, None, 0)
                act_all(act, b1, d0, 0)
                with act.Fori(0, loop) as i:
                    for k in range(4):
                        act_all(act, lb[k], L[3 * k + 2], 12, i)
                for k in range(tail):
                    act_all(act, tb[k], td[k], 0)
                split_hi(act, dl)

            def dve_f(dve):
                dve_all(dve, b0, None, 0)
                dve_all(dve, b1, d0, 0)
                with dve.Fori(0, loop) as i:
                    for k in range(4):
                        dve_all(dve, lb[k], L[3 * k + 2], 12, i)
                for k in range(tail):
                    dve_all(dve, tb[k], td[k], 0)
                split_lo(dve, dl)

            return Part(pe=pe_f, act=act_f, dve=dve_f, acc=acc)


        def narrow(n, loaded, hi_m, lo_m):
            def act_f(act):
                act.wait_ge(loaded, 16)
                nc.scalar.activation(smh[:, :, 0:n], smr[:, :, 0:n], ACT.Copy).then_inc(hi_m.sem, 1)

            def dve_f(dve):
                dve.wait_ge(hi_m.sem, hi_m.value)
                nc.vector.tensor_tensor(sml[:, :, 0:n], smr[:, :, 0:n], f32(smh[:, :, 0:n]),
                                        ALU.subtract).then_inc(lo_m.sem, 1)

            return Part(act=act_f, dve=dve_f)

        def turned_constants():
            use = O[3].use()

            def pe_f(pe):
                constants_built(pe)
                smalls_loaded(pe)
                for g in range(4):
                    n = g_rows[g]
                    ins = pe.transpose(use.ps[:, g * P:g * P + n], stage_rows[0:n, g, :], ident[0:n, 0:n])
                ins.then_inc(use.filled, 1)

            def act_f(act):
                constants_built(act)
                act.wait_ge(use.filled, use.n + 1)
                nc.scalar.activation(fc[:, 0:2 * P + g_rows[2]], use.ps[:, 0:2 * P + g_rows[2]], ACT.Copy)
                nc.scalar.activation(fc[:, 3 * P:3 * P + g_rows[3]], use.ps[:, 3 * P:3 * P + g_rows[3]],
                                     ACT.Copy).then_inc(use.freed, 1)
                act.wait_ge(use.freed, use.n + 1)

            def dve_f(dve):
                constants_built(dve)
                smalls_loaded(dve)
                dve.wait_ge(use.freed, use.n + 1)

            return Part(pe=pe_f, act=act_f, dve=dve_f)

        masks_built = Signal(sem("masks_built"))
        moba_masks, causal_mask = masks_built.next(), masks_built.next()

        def pool_causal(pool, mark):
            for a_, w_, b_ in ((0, P, 0), (P, 2 * P, P)):
                v = fmask[:, a_:a_ + w_]
                nc.gpsimd.affine_select(out=v, in_=v, compare_op=ALU.is_ge, fill=NEG, base=b_,
                                        pattern=[[-1, w_]], channel_multiplier=1)\
                    .then_inc(pool_self.sem, pool_self.add(1))
            pool.wait_ge(pool_self.sem, pool_self.n)
            nc.gpsimd.memset(mx[:, 47:48], 0.0).then_inc(mark.sem, 1)

        def pool_load_memory(pool):
            done = groups_dn[0].on_d[1]
            pool.wait_ge(done.sem, done.value)
            for t in range(NT):
                pool.dma_start(mem_tiles[t], A["mem_2"][0][t * P:(t + 1) * P, :]).then_inc(mem_in, 16)

        def pool_masks_block1(pool):
            last = groups_dn[1].y[1]
            pool.wait_ge(last.sem, last.value)
            pool_tiles(pool, norm_mem)
            nc.gpsimd.iota(fmask[:, 0:P], pattern=[[1, P]], base=0, channel_multiplier=-1,
                           allow_small_or_imprecise_dtypes=True).then_inc(pool_self.sem, pool_self.add(1))
            nc.gpsimd.iota(fmask[:, P:384], pattern=[[1, 2 * P]], base=-P, channel_multiplier=-1,
                           allow_small_or_imprecise_dtypes=True).then_inc(pool_self.sem, pool_self.add(1))
            nc.gpsimd.memset(amask, 0.0).then_inc(pool_self.sem, pool_self.add(1))
            pool.wait_ge(pool_self.sem, pool_self.n)
            nc.gpsimd.memset(amask[0:64, 64:128], NEG).then_inc(pool_self.sem, pool_self.add(1))
            nc.gpsimd.memset(amask[0:64, 320:384], NEG).then_inc(pool_self.sem, pool_self.add(1))
            pool_causal(pool, moba_masks)

        def pool_between_blocks(pool):
            for sem_, value in block1.ready[-1]:
                pool.wait_ge(sem_, value)
            pool.wait_ge(sm_lo.sem, sm_lo.value)
            pool.dma_start(smr[:, :, 0:8], A["w_in_2"][0][:, 3072:3080].rearrange("(k p) n -> p k n", p=P))\
                .then_inc(fg_in, 16)
            nc.gpsimd.memset(fmask, 0.0).then_inc(pool_self.sem, pool_self.add(1))
            pool.wait_ge(pool_self.sem, pool_self.n)
            pool_causal(pool, causal_mask)

        mem_tiles = [qkv[:, f:f + 4, :].rearrange("p f t -> p (f t)") for f in (0, 16)]
        sm1, sm_lo = sm_hi.next(), Signal(sem("narrow_lo_1")).next()
        sm2, sm_lo2 = sm_hi.next(), Signal(sem("narrow_lo_2")).next()

        def pairs(n):
            return [(bhi[:, 2 * k:2 * k + 2, :], blo[:, 2 * k:2 * k + 2, :]) for k in range(n)]

        constants = turned_constants()
        ba_weights = narrow(16, ba_in, sm1, sm_lo)
        norm_dn = transposed_norm([h[:, t, :] for t in range(NT)], A["mix_norm_g"][0:1], lambda t: (x_in, 16), xhi, xlo)
        proj_dn = deltanet_in(norm_dn)
        scalars_dn = deltanet_scalars(proj_dn)
        group0 = deltanet_group(0, scalars_dn.last)
        groups_dn = [group0, deltanet_group(1, group0.last, group0)]
        norm_mem = transposed_norm(mem_tiles, A["norm_mem_2"], lambda t: (mem_in, 16 * NT), bhi[:, 8:16, :],
                                   blo[:, 8:16, :])
        out_dn = rows_gemm(A["dn_w_out"][0], groups_dn[0].parts + groups_dn[1].parts,
                           [[groups_dn[k // 2].y[1].done] for k in range(4)], norm_mem)
        kv0 = memory_block(0, norm_mem)
        add_dn = add_rows(out_dn.acc)
        norm_mlp0 = transposed_norm([h[:, t, :] for t in range(NT)], A["mlp_norm_g"][0:1], add_dn.ready, xhi, xlo)
        mlp0 = mlp(A["mlp_w_up"][0], A["mlp_w_down"][0], norm_mlp0)
        add_mlp0 = add_rows(mlp0.acc)
        kv1 = memory_block(1, norm_mem)
        norm_mb = transposed_norm([h[:, t, :] for t in range(NT)], A["mix_norm_g"][1:2], add_mlp0.ready, xhi, xlo)
        block1 = moba(norm_mb)
        out_mb = rows_gemm(A["mb_w_out"][0], pairs(4), block1.ready)
        add_mb = add_rows(out_mb.acc)
        norm_mlp1 = transposed_norm([h[:, t, :] for t in range(NT)], A["mlp_norm_g"][1:2], add_mb.ready, xhi, xlo)
        mlp1 = mlp(A["mlp_w_up"][1], A["mlp_w_down"][1], norm_mlp1)
        add_mlp1 = add_rows(mlp1.acc)
        kv2, kv3 = memory_block(2, norm_mem), memory_block(3, norm_mem)
        norm_final = norm_in_place(add_mlp1.ready, A["final_norm_g"].rearrange("(a n) -> a n", a=1))
        norm_mix = transposed_norm([h[:, t, :] for t in range(NT)], A["norm_mix_pre_2"], norm_final.ready, xhi, xlo)
        fg_weights = narrow(8, fg_in, sm2, sm_lo2)
        gates = forget_gates(norm_mix)
        mix = block2(norm_mix, gates)
        add_mix = add_normed_rows(mix.acc, A["norm_mix_post_2"])
        norm_cross = transposed_norm([h[:, t, :] for t in range(NT)], A["norm_x_pre_2"], add_mix.ready, xhi, xlo)
        cross = cross_attention(norm_cross, kv3)
        out_cross = rows_gemm(A["w_xo_2"][0], pairs(2), cross.ready)
        add_cross = add_normed_rows(out_cross.acc, A["norm_x_post_2"])
        norm_ffn = transposed_norm([h[:, t, :] for t in range(NT)], A["norm_ffn_pre_2"], add_cross.ready, xhi, xlo)
        ffn = conv_mlp(norm_ffn)
        out_rows = add_normed_rows(ffn.acc, A["norm_ffn_post_2"])
        total_units = state["U"]

        block = ctx.enter_context(nc.Block())

        @block.sync
        def _(sp):
            for n, item in enumerate(stream):
                if n == RAW:
                    for dst, src in small:
                        sp.dma_start(dst, src).then_inc(const_in, 16)
                if item[0] == "unit":
                    load(sp, item[1], item[2])
                else:
                    _, U, iterations, srcs = item
                    with sp.Fori(0, iterations) as i:
                        for k, src in enumerate(srcs):
                            load(sp, U + k, src(i), len(srcs), i)
            o_r = out[0].rearrange("(t p) n -> p t n", p=P)
            for t in range(NT):
                sp.wait_ge(*out_rows.ready(t))
                sp.dma_start(o_r[:, t, :], h[:, t, :]).then_inc(out_done, 16)
            sp.wait_ge(out_done, 16 * NT)

        @block.scalar
        def _(act):
            act.dma_start(h[:, :, :], A["x"][0].rearrange("(t p) n -> p t n", p=P)).then_inc(x_in, 16)
            act.dma_start(smr[:, :, :], A["dn_w_in"][0][:, 4096:4112].rearrange("(k p) n -> p k n", p=P))\
                .then_inc(ba_in, 16)
            act_tiles(act, norm_dn)
            split_hi(act, -3)
            norm_dn.act_parts(act)
            ba_weights.act(act)
            split_hi(act, -2)
            split_hi(act, -1)
            constants.act(act)
            proj_dn.act(act)
            scalars_dn.act(act)
            groups_dn[0].act(act)
            groups_dn[1].act(act)
            out_dn.act(act)
            act_tiles(act, norm_mlp0)
            kv0.act(act)
            norm_mlp0.act_parts(act)
            mlp0.act(act)
            act_tiles(act, norm_mb)
            kv1.act(act)
            norm_mb.act_parts(act)
            block1.act(act)
            out_mb.act(act)
            act_tiles(act, norm_mlp1)
            norm_mlp1.act_parts(act)
            mlp1.act(act)
            act_tiles(act, norm_final, norm_mix)
            kv2.act(act)
            kv3.act(act)
            norm_mix.act_parts(act)
            fg_weights.act(act)
            gates.act(act)
            mix.act(act)
            act_tiles_of_two(act, add_mix, norm_cross)
            norm_cross.act_parts(act)
            cross.act(act)
            out_cross.act(act)
            act_tiles_of_two(act, add_cross, norm_ffn)
            norm_ffn.act_parts(act)
            ffn.act(act)
            act_tiles(act, out_rows)

        @block.vector
        def _(dve):
            dve_tiles(dve, norm_dn)
            split_lo(dve, -3)
            norm_dn.dve_parts(dve)
            ba_weights.dve(dve)
            split_lo(dve, -2)
            split_lo(dve, -1)
            constants.dve(dve)
            proj_dn.dve(dve)
            scalars_dn.dve(dve)
            groups_dn[0].dve(dve)
            groups_dn[1].dve(dve)
            out_dn.dve(dve)
            dve_tiles(dve, add_dn, norm_mlp0)
            kv0.dve(dve)
            norm_mlp0.dve_parts(dve)
            mlp0.dve(dve)
            dve_tiles(dve, add_mlp0, norm_mb)
            kv1.dve(dve)
            norm_mb.dve_parts(dve)
            dve.wait_ge(moba_masks.sem, moba_masks.value)
            block1.dve(dve)
            out_mb.dve(dve)
            dve_tiles(dve, add_mb, norm_mlp1)
            norm_mlp1.dve_parts(dve)
            mlp1.dve(dve)
            dve_tiles(dve, add_mlp1, norm_final, norm_mix)
            kv2.dve(dve)
            kv3.dve(dve)
            norm_mix.dve_parts(dve)
            fg_weights.dve(dve)
            dve.wait_ge(causal_mask.sem, causal_mask.value)
            gates.dve(dve)
            mix.dve(dve)
            dve_tiles_of_two(dve, add_mix, norm_cross)
            norm_cross.dve_parts(dve)
            cross.dve(dve)
            out_cross.dve(dve)
            dve_tiles_of_two(dve, add_cross, norm_ffn)
            norm_ffn.dve_parts(dve)
            ffn.dve(dve)
            dve_tiles(dve, out_rows)

        @block.tensor
        def _(pe):
            constants_built(pe)
            norm_dn.pe(pe)
            constants.pe(pe)
            proj_dn.pe(pe)
            scalars_dn.pe(pe)
            groups_dn[0].pe(pe)
            groups_dn[1].pe(pe)
            out_dn.pe(pe)
            kv0.pe(pe)
            norm_mlp0.pe(pe)
            mlp0.pe(pe)
            kv1.pe(pe)
            norm_mb.pe(pe)
            block1.pe(pe)
            out_mb.pe(pe)
            norm_mlp1.pe(pe)
            mlp1.pe(pe)
            kv2.pe(pe)
            kv3.pe(pe)
            norm_mix.pe(pe)
            gates.pe(pe)
            mix.pe(pe)
            norm_cross.pe(pe)
            cross.pe(pe)
            out_cross.pe(pe)
            norm_ffn.pe(pe)
            ffn.pe(pe)

        @block.gpsimd
        def _(pool):
            load_gain(pool, 0)
            load_gain(pool, 1)
            def build(ins):
                ins.then_inc(pool_self.sem, pool_self.add(1))

            def settled():
                pool.wait_ge(pool_self.sem, pool_self.n)

            def select(ap, op, fill, base, pattern, step):
                build(nc.gpsimd.affine_select(out=ap, in_=ap, compare_op=op, fill=fill, base=base,
                                              pattern=pattern, channel_multiplier=step))

            build(nc.gpsimd.memset(ident[:, :], 0.0))
            build(nc.gpsimd.memset(mhalf[:, :], -0.5))
            settled()
            select(ident[:, :], ALU.not_equal, 1.0, 0, [[-1, P]], 1)
            settled()
            pool.sem_inc(consts_built, 1)
            pool_tiles(pool, norm_dn)
            for ap, v in ((ones[:, :], 1.0), (nones[:, :], -1.0), (upper[:, :], 1.0), (dn_lower[:, :], 1.0),
                          (levels, 0.0)):
                build(nc.gpsimd.memset(ap, v))
            settled()
            halves = []
            for l in range(7):
                s_ = 1 << l
                view = levels[:, l, :].rearrange("p (b h s) -> p b h s", h=2, s=s_)[:, :, 1, :]
                halves.append((s_, view))
                build(nc.gpsimd.memset(view, 1.0))
            select(upper[:, :], ALU.is_ge, 0.0, 0, [[1, P]], -1)
            select(dn_lower[:, :], ALU.is_gt, 0.0, 0, [[-1, P]], 1)
            settled()
            for s_, view in halves:
                select(view, ALU.is_ge, 0.0, 0, [[-2 * s_, P // (2 * s_)], [0, s_]], 1)
            settled()
            for s_, view in halves:
                select(view, ALU.is_ge, 0.0, s_ - 1, [[2 * s_, P // (2 * s_)], [0, s_]], -1)
            settled()
            proj_dn.pool(pool)
            scalars_dn.pool(pool)
            groups_dn[0].pool(pool)
            pool_load_memory(pool)
            groups_dn[1].pool(pool)
            pool_masks_block1(pool)
            pool_tiles(pool, norm_mlp0)
            pool_tiles(pool, norm_mb)
            pool_between_blocks(pool)
            pool_tiles(pool, norm_mlp1)
            pool_tiles(pool, norm_final, norm_mix)
            mix.pool(pool)
            pool_tiles(pool, add_mix, norm_cross)
            pool_tiles(pool, add_cross, norm_ffn)
            pool_tiles(pool, out_rows)


_INS = ["x", "mix_norm_g", "mlp_norm_g", "dn_w_in", "dn_conv_w", "dn_a_log", "dn_dt_bias", "dn_out_norm_g",
        "dn_w_out", "mb_w_in", "mb_w_out", "mlp_w_up", "mlp_w_down", "final_norm_g", "mem_2",
        "norm_mix_pre_2", "norm_mix_post_2", "w_in_2", "b_fgt_2", "lam_q1_2", "lam_k1_2", "lam_q2_2",
        "lam_k2_2", "diff_norm_2", "b_glu_2", "conv_dw_2", "conv_dw_b_2", "conv_ln_g_2", "conv_ln_b_2",
        "sc_w_2", "w_branch_2", "w_gate_2", "b_gate_2", "w_out_2", "norm_x_pre_2", "norm_x_post_2",
        "norm_mem_2", "w_xq_2", "w_xkv_2", "w_xo_2", "norm_ffn_pre_2", "norm_ffn_post_2", "w_up_2",
        "ffn_dw_2", "ffn_dw_b_2", "w_down_2"]


def kernel(**inputs):
    import numpy as _np
    import concourse.bacc as _bacc
    from concourse.bass_utils import run_bass_kernel_spmd as _run

    nc = _bacc.Bacc("TRN2", target_bir_lowering=False, num_devices=1)
    arrays, aps = {}, {}
    for name in _INS:
        a = _np.ascontiguousarray(inputs[name])
        arrays[f"in_{name}"] = a
        aps[name] = nc.dram_tensor(f"in_{name}", a.shape, mybir.dt.from_np(a.dtype), kind="ExternalInput").ap()
    out = nc.dram_tensor("out_0", (1, T, D), F32, kind="ExternalOutput").ap()
    build(nc, aps, out)
    r = _run(nc, [arrays], core_ids=[0])
    return r.results[0]["out_0"]
```
